# Optimizing a Trainium2 kernel written in Bass

```python
import jax
import jax.numpy as jnp
from jax import lax
import numpy as np

D_MODEL = 1024
BATCH = 1
SEQ = 256
DEPTH = 2

HEAD_DIM = 64
NORM_EPS = 1e-6
A_HEADS = 8
A_WIDTH = A_HEADS * HEAD_DIM
A_PATTERNS = ((128, 1), (512, 4), (2048, 16))
A_ROT_DIMS = HEAD_DIM // 4
A_ROPE_THETA = 500000.0
B_Q_HEADS = 8
B_KV_HEADS = 2
B_Q_WIDTH = B_Q_HEADS * HEAD_DIM
B_KV_WIDTH = B_KV_HEADS * HEAD_DIM
B_ROPE_THETA = 10000.0
GRID_W = 64
Q_BLOCK = 128
IN_SPLITS = (A_WIDTH, A_WIDTH, A_WIDTH, B_Q_WIDTH, B_KV_WIDTH, B_KV_WIDTH, D_MODEL, D_MODEL)
IN_COLS = sum(IN_SPLITS)
IN_OFFSETS = tuple(int(v) for v in np.cumsum(IN_SPLITS)[:-1])
N_EXPERTS = 32
N_GROUPS = 4
EXPERTS_PER_GROUP = N_EXPERTS // N_GROUPS
TOP_K = 2
D_FF_EXPERT = D_MODEL // 2
MOE_BLOCK = 256

kernel_name = "hybrid_dilated_gqa_grouped_moe_block"

def rms_norm(x, g):
    xf = x.astype(jnp.float32)
    y = xf * lax.rsqrt(jnp.mean(xf * xf, axis=-1, keepdims=True) + NORM_EPS)
    return (y * g.astype(jnp.float32)).astype(x.dtype)

def modulate(h, shift, scale):
    return h * (1 + scale) + shift

def rope(x, pos, theta):
    half = x.shape[-1] // 2
    freqs = theta ** (-jnp.arange(half, dtype=jnp.float32) / half)
    ang = pos.astype(jnp.float32)[:, None] * freqs
    cos = jnp.cos(ang)[:, None, :]
    sin = jnp.sin(ang)[:, None, :]
    xf = x.astype(jnp.float32)
    x1, x2 = xf[..., :half], xf[..., half:]
    return jnp.concatenate([x1 * cos - x2 * sin, x2 * cos + x1 * sin], axis=-1).astype(x.dtype)

def partial_rope(x, pos):
    return jnp.concatenate([rope(x[..., :A_ROT_DIMS], pos, A_ROPE_THETA), x[..., A_ROT_DIMS:]], axis=-1)

def axial_rope(x, row, col):
    half = x.shape[-1] // 2
    return jnp.concatenate([rope(x[..., :half], row, B_ROPE_THETA), rope(x[..., half:], col, B_ROPE_THETA)], axis=-1)

def dilated_window_attention(q, k, v, dilation, radius):
    B, S, H, E = q.shape
    L = S // dilation
    nb = -(-L // radius)
    Lp = nb * radius

    def strided(a, lo, hi):
        a = a.reshape(B, L, dilation, H, E).transpose(0, 2, 1, 3, 4)
        return jnp.pad(a, ((0, 0), (0, 0), (lo, hi), (0, 0), (0, 0)))

    qs = strided(q, 0, Lp - L).reshape(B, dilation, nb, radius, H, E)

    def band(a):
        a = strided(a, radius, Lp - L + radius).reshape(B, dilation, nb + 2, radius, H, E)
        return jnp.concatenate([a[:, :, :-2], a[:, :, 1:-1], a[:, :, 2:]], axis=3)

    kw, vw = band(k), band(v)
    s = jnp.einsum('bdnqhe,bdnkhe->bdnhqk', qs, kw).astype(jnp.float32) * (E ** -0.5)
    n_idx = jnp.arange(nb)[:, None, None]
    qi = jnp.arange(radius)[None, :, None]
    ki = jnp.arange(3 * radius)[None, None, :]
    kpos = n_idx * radius - radius + ki
    valid = (jnp.abs(ki - radius - qi) <= radius) & (kpos >= 0) & (kpos < L)
    s = jnp.where(valid[:, None], s, -jnp.inf)
    lse = jax.nn.logsumexp(s, axis=-1, keepdims=True)
    p = jnp.exp(s - lse).astype(v.dtype)
    o = jnp.einsum('bdnhqk,bdnkhe->bdnqhe', p, vw).reshape(B, dilation, Lp, H, E)[:, :, :L]
    o = o.transpose(0, 2, 1, 3, 4).reshape(B, S, H, E)
    lse = lse[..., 0].transpose(0, 1, 2, 4, 3).reshape(B, dilation, Lp, H)[:, :, :L]
    lse = lse.transpose(0, 2, 1, 3).reshape(B, S, H)
    return o, lse

def gqa_attention(q, k, v):
    B, S, HQ, E = q.shape
    G = HQ // B_KV_HEADS
    nq = S // Q_BLOCK
    qb = q.reshape(B, nq, Q_BLOCK, B_KV_HEADS, G, E).transpose(1, 0, 2, 3, 4, 5)

    def block(qblk):
        s = jnp.einsum('bqkge,bske->bkgqs', qblk, k).astype(jnp.float32) * (E ** -0.5)
        p = jax.nn.softmax(s, axis=-1).astype(v.dtype)
        return jnp.einsum('bkgqs,bske->bqkge', p, v)

    o = lax.map(block, qb)
    return o.transpose(1, 0, 2, 3, 4, 5).reshape(B, S, HQ * E)

def hybrid_mixer(h, w_in, qn_a, kn_a, qn_b, kn_b, w_pa, w_pb, w_out, pos, row, col):
    B, S, _ = h.shape
    z = h @ w_in
    qa, ka, va, qb, kb, vb, ga, gb = jnp.split(z, IN_OFFSETS, axis=-1)

    def heads(a):
        return a.reshape(B, S, -1, HEAD_DIM)

    qa = partial_rope(rms_norm(heads(qa), qn_a), pos)
    ka = partial_rope(rms_norm(heads(ka), kn_a), pos)
    va = heads(va)
    outs, lses = [], []
    for window, dil in A_PATTERNS:
        o, lse = dilated_window_attention(qa, ka, va, dil, window // (2 * dil))
        outs.append(o)
        lses.append(lse)
    alpha = jax.nn.softmax(jnp.stack(lses), axis=0)
    ya = jnp.einsum('pbsh,pbshe->bshe', alpha, jnp.stack(outs).astype(jnp.float32))
    ya = ya.astype(h.dtype).reshape(B, S, A_WIDTH)

    qb = axial_rope(rms_norm(heads(qb), qn_b), row, col)
    kb = axial_rope(rms_norm(heads(kb), kn_b), row, col)
    yb = gqa_attention(qb, kb, heads(vb))

    merged = jax.nn.sigmoid(ga) * (ya @ w_pa) + jax.nn.sigmoid(gb) * (yb @ w_pb)
    return merged @ w_out

def grouped_moe(h, w_router, w_gate, w_up, w_down):
    B, S, D = h.shape
    T = B * S
    hf = h.reshape(T, D)
    probs = jax.nn.softmax((hf @ w_router).astype(jnp.float32), axis=-1)
    pg = probs.reshape(T, N_GROUPS, EXPERTS_PER_GROUP)
    group_score = lax.top_k(pg, TOP_K)[0].sum(-1)
    g_sel = jnp.argmax(group_score, axis=-1).astype(jnp.int32)
    in_group = pg[jnp.arange(T), g_sel]
    top_w, top_j = lax.top_k(in_group, TOP_K)
    top_e = g_sel[:, None] * EXPERTS_PER_GROUP + top_j.astype(jnp.int32)
    top_w = top_w / jnp.sum(top_w, axis=-1, keepdims=True)

    A = T * TOP_K
    e_flat = top_e.reshape(A)
    tok = jnp.repeat(jnp.arange(T, dtype=jnp.int32), TOP_K)
    wt = top_w.reshape(A)
    order = jnp.argsort(e_flat)
    e_sorted = e_flat[order]
    counts = jnp.zeros((N_EXPERTS,), jnp.int32).at[e_flat].add(1)
    padded = (counts + MOE_BLOCK - 1) // MOE_BLOCK * MOE_BLOCK
    pad_end = jnp.cumsum(padded)
    pad_start = pad_end - padded
    start = jnp.cumsum(counts) - counts
    dest = pad_start[e_sorted] + jnp.arange(A, dtype=jnp.int32) - start[e_sorted]
    n_pad = -(-(A + N_EXPERTS * MOE_BLOCK) // MOE_BLOCK) * MOE_BLOCK
    n_blocks = n_pad // MOE_BLOCK
    buf_tok = jnp.full((n_pad,), T, jnp.int32).at[dest].set(tok[order])
    buf_w = jnp.zeros((n_pad,), jnp.float32).at[dest].set(wt[order])
    blk_e = jnp.minimum(jnp.searchsorted(pad_end, jnp.arange(n_blocks) * MOE_BLOCK, side='right'),
                        N_EXPERTS - 1)
    xb = jnp.concatenate([hf, jnp.zeros((1, D), hf.dtype)], axis=0)[buf_tok]
    xb = xb.reshape(n_blocks, MOE_BLOCK, D)

    def expert_block(args):
        xblk, e = args
        return (jax.nn.silu(xblk @ w_gate[e]) * (xblk @ w_up[e])) @ w_down[e]

    yb = lax.map(expert_block, (xb, blk_e)).reshape(n_pad, D)
    out = jnp.zeros((T + 1, D), h.dtype).at[buf_tok].add(yb * buf_w[:, None].astype(h.dtype))
    return out[:T].reshape(B, S, D)

def setup_inputs(seed: int = 0) -> dict:
    key = jax.random.key(seed)
    ks = jax.random.split(key, 18)

    def nrm(k, shape, scale):
        return jax.random.normal(k, shape, jnp.float32) * scale

    return {
        "x": nrm(ks[0], (BATCH, SEQ, D_MODEL), 1.0),
        "c": nrm(ks[1], (BATCH, D_MODEL), 1.0),
        "w_ada": nrm(ks[2], (DEPTH, D_MODEL, 6 * D_MODEL), 0.5 * D_MODEL ** -0.5),
        "b_ada": nrm(ks[3], (DEPTH, 6 * D_MODEL), 0.02),
        "g_mix": 1.0 + nrm(ks[4], (DEPTH, D_MODEL), 0.02),
        "w_in": nrm(ks[5], (DEPTH, D_MODEL, IN_COLS), D_MODEL ** -0.5),
        "qn_a": 1.0 + nrm(ks[6], (DEPTH, HEAD_DIM), 0.02),
        "kn_a": 1.0 + nrm(ks[7], (DEPTH, HEAD_DIM), 0.02),
        "qn_b": 1.0 + nrm(ks[8], (DEPTH, HEAD_DIM), 0.02),
        "kn_b": 1.0 + nrm(ks[9], (DEPTH, HEAD_DIM), 0.02),
        "w_pa": nrm(ks[10], (DEPTH, A_WIDTH, D_MODEL), A_WIDTH ** -0.5),
        "w_pb": nrm(ks[11], (DEPTH, B_Q_WIDTH, D_MODEL), B_Q_WIDTH ** -0.5),
        "w_out": nrm(ks[12], (DEPTH, D_MODEL, D_MODEL), D_MODEL ** -0.5),
        "g_ffn": 1.0 + nrm(ks[13], (DEPTH, D_MODEL), 0.02),
        "w_router": nrm(ks[14], (D_MODEL, N_EXPERTS), D_MODEL ** -0.5),
        "w_gate": nrm(ks[15], (DEPTH, N_EXPERTS, D_MODEL, D_FF_EXPERT), D_MODEL ** -0.5),
        "w_up": nrm(ks[16], (DEPTH, N_EXPERTS, D_MODEL, D_FF_EXPERT), D_MODEL ** -0.5),
        "w_down": nrm(ks[17], (DEPTH, N_EXPERTS, D_FF_EXPERT, D_MODEL), D_FF_EXPERT ** -0.5),
    }

def reference(x, c, w_ada, b_ada, g_mix, w_in, qn_a, kn_a, qn_b, kn_b, w_pa, w_pb, w_out,
              g_ffn, w_router, w_gate, w_up, w_down):
    B, S, D = x.shape
    pos = jnp.arange(S, dtype=jnp.int32)
    rows = S // GRID_W
    row = jnp.repeat(jnp.arange(rows, dtype=jnp.int32), GRID_W)
    col = jnp.tile(jnp.arange(GRID_W, dtype=jnp.int32), rows)
    cond = jax.nn.silu(c)
    for l in range(DEPTH):
        mod = (cond @ w_ada[l] + b_ada[l])[:, None, :]
        sh1, sc1, gt1, sh2, sc2, gt2 = jnp.split(mod, 6, axis=-1)
        h = modulate(rms_norm(x, g_mix[l]), sh1, sc1)
        x = x + gt1 * hybrid_mixer(h, w_in[l], qn_a[l], kn_a[l], qn_b[l], kn_b[l],
                                   w_pa[l], w_pb[l], w_out[l], pos, row, col)
        h = modulate(rms_norm(x, g_ffn[l]), sh2, sc2)
        x = x + gt2 * grouped_moe(h, w_router, w_gate[l], w_up[l], w_down[l])
    return x


_drawn_inputs = setup_inputs


def setup_inputs(seed=0):
    import zlib

    import numpy as np

    out = dict(_drawn_inputs(seed))
    spreads = {}
    factors = {'g_mix': 5.549, 'qn_a': 8.0, 'kn_a': 5.848, 'qn_b': 8.0, 'kn_b': 5.854}
    for name, (base, spread) in spreads.items():
        noise = np.random.default_rng([zlib.crc32(name.encode()), seed]).standard_normal(out[name].shape)
        drawn = base * np.exp(spread * noise) if base else spread * noise
        out[name] = jnp.asarray(drawn.astype(out[name].dtype))
    for name, factor in factors.items():
        out[name] = (out[name] * factor).astype(out[name].dtype)
    return out
```

```python
from contextlib import ExitStack

import numpy as np

import concourse.bass as bass
from concourse import mybir

ALU = mybir.AluOpType
ACT = mybir.ActivationFunctionType
AX = mybir.AxisListType
F32 = mybir.dt.float32
I32 = mybir.dt.int32

P = 128
D = 1024
T = 256
DEPTH = 2
DC = D // P
TT = T // P
E = 64
HA = 8
KVB = 2
NH = 2 * HA
AW = HA * E
IN_COLS = 3 * AW + AW + 2 * KVB * E + 2 * D
NE = 32
NG = 4
EG = NE // NG
FF = D // 2
FC = FF // P
W = 64
NBLK = T // W
SLOTS = 2 * T
SPAD = SLOTS + W
EPS = 1e-6
QSCALE = E ** -0.5
MASKED = -1e37
RSQRT_MAGIC = 1597463007.0

RING = 6
RW = 4096

C_ID, C_ONE, C_UP, C_MASK = 0, 128, 256, 384
C_COSA, C_SINA = 896, 928
C_COSB, C_SINB = 960, 1088
C_IOTA, C_DESC = 1216, 1728
NCONST = 1736


def constants():
    k = np.zeros((P, NCONST), np.float32)
    k[:, C_ID:C_ID + P] = np.eye(P)
    k[:, C_ONE:C_ONE + P] = 1.0
    k[:, C_UP:C_UP + P] = np.triu(np.ones((P, P)), 1)
    t = np.arange(T)
    gap = np.abs(t[:, None] - t[None, :])
    count = (gap <= 64).astype(int) + (gap % 4 == 0) + (gap % 16 == 0)
    mask = np.where(count > 0, np.log(np.maximum(count, 1)) / QSCALE, MASKED)

    def rotary(pos, half, theta):
        freq = np.float32(theta) ** (-np.arange(half, dtype=np.float32) / np.float32(half))
        ang = (pos.astype(np.float32)[:, None] * freq.astype(np.float32)).astype(np.float32).astype(np.float64)
        cos, sin = np.cos(ang), np.sin(ang)
        return np.concatenate([cos, cos], 1), np.concatenate([-sin, sin], 1)

    ca, sa = rotary(t, 8, 500000.0)
    cr, sr = rotary(t // 64, 16, 10000.0)
    cc, sc = rotary(t % 64, 16, 10000.0)
    cb, sb = np.concatenate([cr, cc], 1), np.concatenate([sr, sc], 1)
    for n in range(TT):
        rows = slice(n * P, (n + 1) * P)
        k[:, C_MASK + n * T:C_MASK + (n + 1) * T] = mask[rows]
        k[:, C_COSA + n * 16:C_COSA + (n + 1) * 16] = ca[rows]
        k[:, C_SINA + n * 16:C_SINA + (n + 1) * 16] = sa[rows]
        k[:, C_COSB + n * E:C_COSB + (n + 1) * E] = cb[rows]
        k[:, C_SINB + n * E:C_SINB + (n + 1) * E] = sb[rows]
    k[:, C_IOTA:C_IOTA + SLOTS] = np.arange(SLOTS)
    k[:, C_DESC:C_DESC + EG] = EG - np.arange(EG)
    return k


ADA = [(l, j, kh) for l in range(DEPTH) for j in range(6) for kh in range(2)]
BATCH = [(0, 4), (4, 12), (12, 24)]
Z_KINDS = ["qa", "ka", "kb", "qb", "va"]
ZN = [(k, t) for k in Z_KINDS for t in range(TT)]
QN = [(k, t) for k in ("qa", "ka", "kb", "qb") for t in range(TT)]
Z_COLS = {"qa": (0, 512), "ka": (512, 512), "va": (1024, 512), "qb": (1536, 512), "kb": (2048, 256)}
GATE_COL = IN_COLS - 2 * D


def filler(l, h):
    q, r = divmod(h, 4)
    if l == 0:
        a = 4 + 5 * q
        return [[("gate", 4 * q), ("gate", 4 * q + 1)],
                [("gate", 4 * q + 2), ("gate", 4 * q + 3), ("ada", a)],
                [("ada", a + 1), ("ada", a + 2)],
                [("ada", a + 3), ("ada", a + 4)]][r]
    return [("gate", h)]


def weight_items():
    items = [("ada", n) for n in range(4)]
    for l in range(DEPTH):
        items += [("z", l, k) for k in Z_KINDS]
        for h in range(NH):
            for f in filler(l, h):
                if f[0] == "ada":
                    items.append(f)
                elif f[1] % 4 == 0:
                    items.append(("gate", l, f[1] // 4))
        items += [("pa", l), ("pb", l), ("out", l, 0), ("out", l, 1)]
        items += [(w, l, e) for e in range(NE) for w in ("wg", "wu", "wd")]
    return items


def psum_groups():
    g = [("XT", q) for q in range(4)]
    for l in range(DEPTH):
        g += [("MS", l, 0), ("RB", l, 0)]
        for n, k in enumerate(Z_KINDS):
            g += [("Z", l, k, t) for t in range(TT)]
            if n:
                g += [("QT", l, Z_KINDS[n - 1], t) for t in range(TT)]
        for h in range(NH + 1):
            if h < NH:
                g.append(("S", l, h))
            if h >= 1:
                g.append(("PT", l, h - 1))
            if h < NH:
                for f in filler(l, h):
                    if f[0] == "gate" and f[1] % 2 == 0:
                        g.append(("G", l, f[1] // 2))
            if h >= 1:
                if (h - 1) % 4 == 0:
                    g.append(("O", l, (h - 1) // 4))
                if (h - 1) % 4 == 3:
                    g.append(("YT", l, (h - 1) // 4))
        for n in ("PA", "PB", "OUT"):
            g += [(n, l, q) for q in range(4)]
        g += [("MS", l, 1), ("RB", l, 1)]
        g += [("RT", l)] + [("H2", l, q) for q in range(4)]
        g += [("CNT", l), ("START", l), ("POS", l)]
        g += [("XS", l, c) for c in range(DC)] + [("WT", l, q) for q in range(2)]
        g += [("MOE", l)]
        g += [("YS", l, q) for q in range(8)] + [("CMB", l, q) for q in range(4)]
    g += [("FIN", q) for q in range(4)]
    return g


NBANK = 7


def plan_banks():
    place, before, owner, full = {}, {}, [None] * NBANK, [0] * NBANK
    n = 0
    for g in psum_groups():
        if g[0] == "MOE":
            before[g] = [o for o in owner[:6] if o is not None]
            for b in range(6):
                owner[b] = g
            n = 0
            continue
        if g[0] == "O":
            b = NBANK - 1
        else:
            b = n % (NBANK - 1)
            n += 1
        before[g] = [owner[b]] if owner[b] is not None else []
        full[b] += 1
        place[g] = (b, full[b])
        owner[b] = g
    return place, before


def build(nc, x, c, w_ada, b_ada, g_mix, w_in, qn_a, kn_a, qn_b, kn_b, w_pa, w_pb, w_out, g_ffn,
          w_router, w_gate, w_up, w_down, const, out, overflow_at=W):
    place, before = plan_banks()
    items = weight_items()
    index = {it: n for n, it in enumerate(items)}

    ctx = ExitStack()
    with ctx:
        def sb(name, shape, dt=F32):
            return ctx.enter_context(nc.sbuf_tensor(name, shape, dt))

        def sem(name):
            return ctx.enter_context(nc.semaphore(name))

        ring = sb("ring", [P, RING, RW])
        xT = sb("xT", [P, DC, T])
        hT = sb("hT", [P, DC, T])
        con = sb("con", [P, NCONST])
        g_sb = sb("g_sb", [P, 2, DEPTH, DC])
        qk_gain = sb("qk_gain", [P, 4, DEPTH, E])
        b_sb = sb("b_sb", [P, DEPTH, 6, DC])
        wr_sb = sb("wr_sb", [P, DC, NE])
        c_sb = sb("c_sb", [P, DC])
        cond = sb("cond", [P, DC])
        mod = sb("mod", [P, DEPTH, 6, DC])
        mscale = sb("mscale", [P, DEPTH, 2, DC])
        ghalf = sb("ghalf", [P, DEPTH, DC])
        nw = sb("nw", [P, 4, 8])
        rstd = sb("rstd", [P, 8])
        diag = sb("diag", [P, TT, P])
        ccol = sb("ccol", [NE, P])
        tables = [sb(f"table{l}", [1, NBLK * NE + 1], I32) for l in range(DEPTH)]
        mx = sb("mx", [P, 2, TT])
        nmax = sb("nmax", [P, 2, TT])
        den = sb("den", [P, 2, TT, 4])
        rden = sb("rden", [P, 2, TT, 4])

        WORK = 20224
        work = sb("work", [P, WORK])
        at = [0]

        def part(n):
            a = work[:, at[0]:at[0] + n]
            at[0] += n
            assert at[0] <= WORK
            return a

        va = part(TT * AW).rearrange("p (t n) -> p t n", t=TT)
        vb = part(TT * KVB * E).rearrange("p (t n) -> p t n", t=TT)
        qT = {"qa": part(4 * T).rearrange("p (c t) -> p c t", c=4),
              "ka": part(4 * T).rearrange("p (c t) -> p c t", c=4),
              "qb": part(4 * T).rearrange("p (c t) -> p c t", c=4),
              "kb": part(2 * T).rearrange("p (c t) -> p c t", c=2)}
        zsq = part(2 * AW).rearrange("p (b n) -> p b n", b=2)
        zraw = part(2 * AW).rearrange("p (b n) -> p b n", b=2)
        zq = part(2 * AW).rearrange("p (b n) -> p b n", b=2)
        ztmp = part(2 * AW).rearrange("p (b n) -> p b n", b=2)
        gth = part(2 * DC * T).rearrange("p (b c t) -> p b c t", b=2, c=DC)
        ybr = part(2 * TT * AW).rearrange("p (b t n) -> p b t n", b=2, t=TT)
        yT = part(2 * 4 * T).rearrange("p (b c t) -> p b c t", b=2, c=4)
        sm = part(2 * TT * T).rearrange("p (b t n) -> p b t n", b=2, t=TT)
        pr = part(2 * TT * T).rearrange("p (b t n) -> p b t n", b=2, t=TT)
        pT = part(2 * TT * T).rearrange("p (b t n) -> p b t n", b=2, t=TT)
        at[0] = 0
        xs = part(DC * SPAD).rearrange("p (c s) -> p c s", c=DC)
        ys = part(DC * SPAD).rearrange("p (c s) -> p c s", c=DC)
        sel_s = part(TT * SLOTS).rearrange("p (t s) -> p t s", t=TT)
        sel_w = part(TT * SLOTS).rearrange("p (t s) -> p t s", t=TT)
        sel_t = part(TT * SLOTS).rearrange("p (t s) -> p t s", t=TT)
        h2 = part(TT * D).rearrange("p (t c n) -> p t c n", t=TT, c=DC)
        wT = part(4 * T).rearrange("p (s t) -> p s t", s=4)
        xblk = part(2 * DC * W).rearrange("p (b c s) -> p b c s", b=2, c=DC)
        th = part(2 * FC * W).rearrange("p (b f s) -> p b f s", b=2, f=FC)
        sw = part(2 * FC * W).rearrange("p (b f s) -> p b f s", b=2, f=FC)
        hb = part(2 * FC * W).rearrange("p (b f s) -> p b f s", b=2, f=FC)
        rt = part(24 * TT * NE).rearrange("p (r n) -> p r n", r=24)
        yd = work[:, 0:4 * D].rearrange("p (s d) -> p s d", s=4)
        xin = work[:, 0:TT * D].rearrange("p (t d) -> p t d", t=TT)
        fin = work[:, 4096:4096 + TT * D].rearrange("p (t n c) -> p t n c", t=TT, c=DC)

        ident = con[:, C_ID:C_ID + P]
        ones = con[:, C_ONE:C_ONE + P]
        upper = con[:, C_UP:C_UP + P]
        iota = con[:, C_IOTA:C_IOTA + SLOTS]
        desc = con[:, C_DESC:C_DESC + EG]

        bank = [ctx.enter_context(nc.psum_tensor(f"bank{b}", [P, 512], F32)) for b in range(8)]
        ada_ps = bank[7]

        def ps(g):
            return bank[place[g][0]]

        landed = [sem(f"weights_landed{s}") for s in range(RING)]
        full = [sem(f"bank_full{b}") for b in range(NBANK)]
        s_in = [sem(f"input_landed{n}") for n in range(14)]
        s_xT = sem("xT_chunk_ready")
        s_cexp = sem("cond_tanh")
        s_cond = sem("cond_ready")
        s_ada = sem("ada_item_used")
        s_mod = sem("mod_ready")
        s_sq = sem("squares_ready")
        s_ms = sem("mean_square_taken")
        s_diag = sem("rstd_diag_ready")
        s_hn = sem("h_normed")
        s_h = sem("h_ready")
        s_z = sem("z_copied")
        s_zq = sem("qk_roped")
        s_qT = sem("qkT_ready")
        s_smx = sem("scores_masked")
        s_nm = sem("neg_max_ready")
        s_exp = sem("probs_ready")
        s_pv = sem("values_done")
        s_pT = sem("probsT_ready")
        s_y = sem("branch_quad_ready")
        s_yT = sem("branchT_quad_ready")
        s_g = sem("gate_tanh_ready")
        s_ma = sem("branch_a_gated")
        s_mb = sem("branch_b_gated")
        s_m = sem("merged_ready")
        s_out0 = sem("w_out_first_half_used")
        s_x1 = sem("x_after_mixer")
        s_rmax = sem("router_max_ready")
        s_rexp = sem("router_exp_ready")
        s_sel = sem("selection_ready")
        s_cnt = sem("counts_copied")
        s_start = sem("starts_copied")
        s_tab = sem("table_ready")
        s_slot = sem("slots_taken")
        s_S = sem("gather_matrix_ready")
        s_Wm = sem("combine_matrix_ready")
        s_h2 = sem("h_token_major_ready")
        s_pad = sem("xs_pad_cleared")
        s_xsa = sem("xs_even_ready")
        s_xsv = sem("xs_odd_ready")
        s_wT = sem("combineT_ready")
        s_xb = sem("expert_tokens_ready")
        s_gd = sem("expert_gate_done")
        s_ud = sem("expert_up_done")
        s_yd = sem("expert_down_done")
        s_th = sem("expert_tanh_ready")
        s_sw = sem("expert_swish_ready")
        s_hb = sem("expert_hidden_ready")
        s_ys = sem("expert_result_stored")
        s_yea = sem("results_even_copied")
        s_yev = sem("results_odd_copied")
        s_x2 = sem("x_after_experts")
        s_fin = sem("output_ready")
        s_out = sem("output_stored")
        s_link = sem("dve_step")
        fb = [{n: sem(f"over{l}_{n}") for n in ("landed", "x", "up", "down", "tanh", "swish", "h", "ys")}
              for l in range(DEPTH)]

        XC = [s_xsa, s_xsv]

        def released(g):
            k, r = g[0], g[1:]
            if k == "XT":
                return [(s_xT, r[0] + 1)]
            if k == "FIN":
                return [(s_fin, r[0] + 1)]
            l = r[0]
            if k == "MS":
                return [(s_ms, 2 * l + r[1] + 1)]
            if k == "RB":
                return [(s_hn, 2 * l + r[1] + 1)]
            if k == "Z":
                return [(s_z, 10 * l + ZN.index(r[1:]) + 1)]
            if k == "QT":
                return [(s_qT, 8 * l + QN.index(r[1:]) + 1)]
            if k == "S":
                return [(s_exp, NH * l + r[1] + 1)]
            if k == "PT":
                return [(s_pT, NH * l + r[1] + 1)]
            if k == "G":
                return [(s_g, 8 * l + r[1] + 1)]
            if k == "O":
                return [(s_y, 4 * l + r[1] + 1)]
            if k == "YT":
                return [(s_yT, 4 * l + r[1] + 1)]
            if k == "PA":
                return [(s_ma, 4 * l + r[1] + 1)]
            if k == "PB":
                return [(s_mb, 4 * l + r[1] + 1)]
            if k == "OUT":
                return [(s_x1, 8 * l + 2 * r[1] + 2)]
            if k == "RT":
                return [(s_rexp, l + 1)]
            if k == "H2":
                return [(s_h2, 4 * l + r[1] + 1)]
            if k == "CNT":
                return [(s_cnt, l + 1)]
            if k == "START":
                return [(s_tab, l + 1)]
            if k == "POS":
                return [(s_slot, l + 1)]
            if k == "XS":
                return [(XC[r[1] % 2], 4 * l + r[1] // 2 + 1)]
            if k == "WT":
                return [(s_wT, 2 * l + r[1] + 1)]
            if k == "MOE":
                return [(s_hb, NE * (l + 1)), (s_ys, NE * (l + 1))]
            if k == "YS":
                return [((s_yea, s_yev)[r[1] % 2], 4 * l + r[1] // 2 + 1)]
            assert k == "CMB"
            return [(s_x2, 8 * l + 2 * r[1] + 2)]

        def bank_wait(pe, g):
            for o in before[g]:
                for s, v in released(o):
                    pe.wait_ge(s, v)

        def full_wait(eng, g):
            b, v = place[g]
            eng.wait_ge(full[b], v)

        def full_inc(ins, g):
            ins.then_inc(full[place[g][0]], 1)

        def used(it):
            k = it[0]
            if k == "ada":
                return s_ada, it[1] + 1
            l = it[1]
            if k in ("wg", "wu", "wd"):
                return {"wg": s_gd, "wu": s_ud, "wd": s_yd}[k], NE * l + it[2] + 1
            if k == "out" and it[2] == 0:
                return s_out0, l + 1
            g = {"z": lambda: ("Z", l, it[2], TT - 1), "gate": lambda: ("G", l, 2 * it[2] + 1),
                 "pa": lambda: ("PA", l, 3), "pb": lambda: ("PB", l, 3), "out": lambda: ("OUT", l, 3)}[k]()
            b, v = place[g]
            return full[b], v

        def slot_of(it):
            return index[it] % RING

        def weights_wait(eng, it):
            n = index[it]
            eng.wait_ge(landed[n % RING], 16 * (n // RING + 1))

        def rows_8p(w):
            return w.rearrange("(p c) n -> p c n", p=P)

        def rows_128c(w):
            return w.rearrange("(c p) n -> p c n", p=P)

        def expert_src(k, l, e):
            w = {"wg": w_gate, "wu": w_up, "wd": w_down}[k][l]
            w = w[e] if isinstance(e, int) else w[bass.ds(e, 1)].rearrange("a r n -> (a r) n")
            return rows_128c(w) if k == "wd" else rows_8p(w)

        def load(eng, it, signal=None):
            k = it[0]
            s = slot_of(it)
            buf = ring[:, s, :]
            if k == "ada":
                l, j, kh = ADA[it[1]]
                src = rows_8p(w_ada[l])[:, 4 * kh:4 * kh + 4, j * D:(j + 1) * D]
                dst = buf.rearrange("p (c n) -> p c n", c=4)
            elif k == "z":
                a, n = Z_COLS[it[2]]
                src = rows_8p(w_in[it[1]])[:, :, a:a + n]
                dst = buf[:, 0:DC * n].rearrange("p (c n) -> p c n", c=DC)
            elif k == "gate":
                a = GATE_COL + it[2] * 512
                src = rows_8p(w_in[it[1]])[:, :, a:a + 512]
                dst = buf.rearrange("p (c n) -> p c n", c=DC)
            elif k in ("pa", "pb"):
                src = rows_128c((w_pa if k == "pa" else w_pb)[it[1]])
                dst = buf.rearrange("p (c n) -> p c n", c=4)
            elif k == "out":
                src = rows_128c(w_out[it[1]])[:, 4 * it[2]:4 * it[2] + 4, :]
                dst = buf.rearrange("p (c n) -> p c n", c=4)
            else:
                src = expert_src(*it)
                dst = buf.rearrange("p (c n) -> p c n", c=4 if k == "wd" else DC)
            eng.dma_start(dst, src).then_inc(signal or landed[s], 16)

        small = [
            (xin[:, :, :], x[0].rearrange("(t p) d -> p t d", p=P)),
            (con[:, :], const),
            (c_sb[:, :], c[0].rearrange("(p c) -> p c", p=P)),
            (b_sb[:, :, :, :], b_ada.rearrange("l (j p c) -> p l j c", j=6, p=P)),
            (g_sb[:, 0], g_mix.rearrange("l (p c) -> p l c", p=P)),
            (g_sb[:, 1], g_ffn.rearrange("l (p c) -> p l c", p=P)),
            (qk_gain[:, 0], qn_a.partition_broadcast(P)),
            (qk_gain[:, 1], kn_a.partition_broadcast(P)),
            (qk_gain[:, 2], qn_b.partition_broadcast(P)),
            (qk_gain[:, 3], kn_b.partition_broadcast(P)),
            (wr_sb[:, :, :], w_router.rearrange("(p c) e -> p c e", p=P)),
        ]
        IN_X, IN_CON, IN_C, IN_B, IN_G, IN_QK, IN_WR = 0, 1, 2, 3, 4, 6, 10

        block = ctx.enter_context(nc.Block())

        @block.sync
        def _(sp):
            def stream(n):
                if n >= RING:
                    sp.wait_ge(*used(items[n - RING]))
                load(sp, items[n])

            n = 0
            for l in range(DEPTH):
                first = index[("wg", l, 0)]
                while n < first + 6:
                    stream(n)
                    n += 1
                with sp.Fori(1, NE // 2) as i:
                    for j in range(6):
                        k, _, e0 = items[first + j]
                        sp.wait_ge(used((k, l, e0))[0], i * 2 + (NE * l + e0 - 1))
                        s = (first + j) % RING
                        sp.dma_start(ring[:, s, :].rearrange("p (c n) -> p c n", c=4 if k == "wd" else DC),
                                     expert_src(k, l, i * 2 + e0)).then_inc(landed[s], 16)
                n = first + 3 * NE
                sp.wait_ge(s_tab, l + 1)
                count = sp.value_load(tables[l][0:1, NBLK * NE:NBLK * NE + 1], min_val=0, max_val=T)
                with sp.If(count > overflow_at):
                    f = fb[l]
                    with sp.Fori(0, NE) as e:
                        sp.wait_ge(f["down"], e * NBLK + 1)
                        for j, k in enumerate(("wg", "wu", "wd")):
                            sp.dma_start(ring[:, j, :].rearrange("p (c n) -> p c n", c=4 if k == "wd" else DC),
                                         expert_src(k, l, e)).then_inc(f["landed"], 16)
                    sp.wait_ge(f["down"], NE * NBLK + 1)
            sp.wait_ge(s_out, 16)

        @block.gpsimd
        def _(pool):
            for n, (dst, src) in enumerate(small):
                pool.dma_start(dst, src).then_inc(s_in[n], 16)
            for l in range(DEPTH):
                pool.wait_ge(s_x1, 8 * (l + 1))
                pool.memset(xs[:, :, SLOTS:SPAD], 0.0).then_inc(s_pad, 1)
                pool.wait_ge(s_pad, l + 1)
                pool.wait_ge(s_tab, l + 1)
                for s in XC:
                    pool.wait_ge(s, 4 * (l + 1))

                def tokens(e, j, steady):
                    if steady:
                        pool.wait_ge(s_ud, e + (NE * l - 1))
                    first = pool.value_load(tables[l][0:1, bass.ds(e, 1)] if steady else tables[l][0:1, e:e + 1],
                                            min_val=0, max_val=SLOTS)
                    pool.tensor_copy(xblk[:, j], xs[:, :, bass.ds(first, W)]).then_inc(s_xb, 1)

                for j in range(2):
                    tokens(j, j, False)
                with pool.Fori(1, NE // 2) as i:
                    for j in range(2):
                        tokens(i * 2 + j, j, True)
                count = pool.value_load(tables[l][0:1, NBLK * NE:NBLK * NE + 1], min_val=0, max_val=T)
                with pool.If(count > overflow_at):
                    f = fb[l]
                    pool.wait_ge(s_ud, NE * (l + 1))
                    with pool.Fori(0, NE) as e:
                        for b in range(NBLK):
                            pool.wait_ge(f["up"], e * NBLK + (b + 1))
                            first = pool.value_load(tables[l][0:1, bass.ds(e + b * NE, 1)], min_val=0, max_val=SLOTS)
                            pool.tensor_copy(xblk[:, 0], xs[:, :, bass.ds(first, W)]).then_inc(f["x"], 1)

        @block.scalar
        def _(act):
            act.wait_ge(s_in[IN_C], 16)
            act.activation(cond[:, :], c_sb[:, :], ACT.Tanh, scale=0.5).then_inc(s_cexp, 1)
            for q in range(4):
                full_wait(act, ("XT", q))
                act.activation(xT[:, 2 * q:2 * q + 2, :], ps(("XT", q))[:, :].rearrange("p (c t) -> p c t", c=2),
                               ACT.Copy).then_inc(s_xT, 1)

            def squares(l, w):
                if l == 0 and w == 0:
                    act.wait_ge(s_xT, 4)
                elif w == 0:
                    act.wait_ge(s_x2, 8 * l)
                else:
                    act.wait_ge(s_x1, 8 * (l + 1))
                act.activation(hT[:, :, :], xT[:, :, :], ACT.Square).then_inc(s_sq, 1)

            def z_out(l, n):
                k, t = ZN[n]
                g = ("Z", l, k, t)
                full_wait(act, g)
                if k == "va":
                    act.activation(va[:, t, :], ps(g)[:, :], ACT.Copy).then_inc(s_z, 1)
                    return
                q = 8 * l + QN.index((k, t))
                if q >= 2:
                    act.wait_ge(s_zq, q - 1)
                m = 128 if k == "kb" else 512
                if k == "kb":
                    act.activation(vb[:, t, :], ps(g)[:, 128:256], ACT.Copy)
                act.activation(zsq[:, q % 2, 0:m], ps(g)[:, 0:m], ACT.Square)
                act.activation(zraw[:, q % 2, 0:m], ps(g)[:, 0:m], ACT.Copy).then_inc(s_z, 1)

            def qT_out(l, k, t):
                g = ("QT", l, k, t)
                n = 2 if k == "kb" else 4
                full_wait(act, g)
                act.activation(qT[k][:, :, t * P:(t + 1) * P],
                               ps(g)[:, 0:n * P].rearrange("p (c t) -> p c t", c=n), ACT.Copy).then_inc(s_qT, 1)

            def exps(l, h):
                b = h % 2
                n = NH * l + h
                act.wait_ge(s_nm, n + 1)
                if h >= 2:
                    full_wait(act, ("PT", l, h - 2))
                if h % 4 == 0 and h >= 8:
                    act.wait_ge(s_y, 4 * l + h // 4 - 1)
                for t in range(TT):
                    src = sm[:, b, t, :] if h < HA else ps(("S", l, h))[:, t * T:(t + 1) * T]
                    ins = act.activation(pr[:, b, t, :], src, ACT.Exp, bias=nmax[:, b, t:t + 1], scale=QSCALE,
                                         accum_out=den[:, (h // 4) % 2, t, h % 4:h % 4 + 1])
                ins.then_inc(s_exp, 1)

            def gates(l, p):
                g = ("G", l, p)
                full_wait(act, g)
                act.activation(gth[:, p // 4, 2 * (p % 4):2 * (p % 4) + 2, :],
                               ps(g)[:, :].rearrange("p (c t) -> p c t", c=2), ACT.Tanh, scale=0.5).then_inc(s_g, 1)

            def yT_out(l, q):
                g = ("YT", l, q)
                full_wait(act, g)
                act.activation(yT[:, q // 2, 2 * (q % 2):2 * (q % 2) + 2, :],
                               ps(g)[:, :].rearrange("p (c t) -> p c t", c=2), ACT.Copy).then_inc(s_yT, 1)

            for l in range(DEPTH):
                squares(l, 0)
                for n, k in enumerate(Z_KINDS):
                    for t in range(TT):
                        z_out(l, n * TT + t)
                    if n:
                        for t in range(TT):
                            qT_out(l, Z_KINDS[n - 1], t)
                for h in range(NH + 1):
                    if h < NH:
                        exps(l, h)
                        for f in filler(l, h):
                            if f[0] == "gate" and f[1] % 2 == 1:
                                gates(l, f[1] // 2)
                    if h >= 1 and (h - 1) % 4 == 3:
                        yT_out(l, (h - 1) // 4)
                squares(l, 1)
                act.wait_ge(s_rmax, l + 1)
                for t in range(TT):
                    ins = act.activation(rt[:, 0, t * NE:(t + 1) * NE], ps(("RT", l))[:, t * NE:(t + 1) * NE], ACT.Exp,
                                         bias=rt[:, 1, t:t + 1], scale=1.0, accum_out=rt[:, 2, t:t + 1])
                ins.then_inc(s_rexp, 1)
                for q in range(4):
                    g = ("H2", l, q)
                    full_wait(act, g)
                    act.activation(h2[:, q // 2, 4 * (q % 2):4 * (q % 2) + 4, :],
                                   ps(g)[:, :].rearrange("p (c n) -> p c n", c=4), ACT.Copy).then_inc(s_h2, 1)
                for cc in range(0, DC, 2):
                    g = ("XS", l, cc)
                    full_wait(act, g)
                    act.activation(xs[:, cc, 0:SLOTS], ps(g)[:, :], ACT.Copy).then_inc(s_xsa, 1)
                for q in range(2):
                    g = ("WT", l, q)
                    full_wait(act, g)
                    act.activation(wT[:, 2 * q:2 * q + 2, :], ps(g)[:, :].rearrange("p (s t) -> p s t", s=2),
                                   ACT.Copy).then_inc(s_wT, 1)

                act.wait_ge(s_tab, l + 1)

                def tanh_gate(e, j, steady):
                    act.wait_ge(s_gd, e + (NE * l + 1))
                    if steady:
                        act.wait_ge(s_sw, e + (NE * l - 1))
                    act.activation(th[:, j], bank[3 * j][:, 0:FC * W].rearrange("p (f s) -> p f s", f=FC),
                                   ACT.Tanh, scale=0.5).then_inc(s_th, 1)

                def store(e, j, steady):
                    first = act.value_load(tables[l][0:1, bass.ds(e, 1)] if steady else tables[l][0:1, e:e + 1],
                                           min_val=0, max_val=SLOTS)
                    act.wait_ge(s_yd, e + (NE * l + 1))
                    act.wait_ge(s_ys, e + NE * l)
                    act.activation(ys[:, :, bass.ds(first, W)],
                                   bank[3 * j + 2][:, :].rearrange("p (c s) -> p c s", c=DC), ACT.Copy).then_inc(s_ys, 1)

                for j in range(2):
                    tanh_gate(j, j, False)
                    store(j, j, False)
                with act.Fori(1, NE // 2) as i:
                    for j in range(2):
                        tanh_gate(i * 2 + j, j, True)
                        store(i * 2 + j, j, True)
                count = act.value_load(tables[l][0:1, NBLK * NE:NBLK * NE + 1], min_val=0, max_val=T)
                with act.If(count > overflow_at):
                    f = fb[l]
                    act.wait_ge(s_ys, NE * (l + 1))
                    act.sem_inc(f["ys"], 1)
                    with act.Fori(0, NE) as e:
                        for b in range(NBLK):
                            act.wait_ge(f["up"], e * NBLK + (b + 2))
                            act.activation(th[:, 0], bank[0][:, 0:FC * W].rearrange("p (f s) -> p f s", f=FC),
                                           ACT.Tanh, scale=0.5).then_inc(f["tanh"], 1)
                            first = act.value_load(tables[l][0:1, bass.ds(e + b * NE, 1)], min_val=0, max_val=SLOTS)
                            act.wait_ge(f["down"], e * NBLK + (b + 2))
                            act.activation(ys[:, :, bass.ds(first, W)],
                                           bank[2][:, :].rearrange("p (c s) -> p c s", c=DC),
                                           ACT.Copy).then_inc(f["ys"], 1)
                            act.wait_ge(f["ys"], e * NBLK + (b + 2))
                for q in range(0, 8, 2):
                    g = ("YS", l, q)
                    full_wait(act, g)
                    act.activation(yd[:, q // 2, 0:512], ps(g)[:, :], ACT.Copy).then_inc(s_yea, 1)
            for q in range(4):
                g = ("FIN", q)
                full_wait(act, g)
                act.activation(fin[:, q // 2, :, 4 * (q % 2):4 * (q % 2) + 4].rearrange("p n c -> p c n"),
                               ps(g)[:, :].rearrange("p (c n) -> p c n", c=4), ACT.Copy).then_inc(s_fin, 1)
            act.wait_ge(s_fin, 4)
            act.dma_start(out[0].rearrange("(t p) d -> p t d", p=P),
                          work[:, 4096:4096 + TT * D].rearrange("p (t d) -> p t d", t=TT)).then_inc(s_out, 16)
            act.wait_ge(s_out, 16)

        @block.vector
        def _(dve):
            steps = [0]

            def link(ins):
                steps[0] += 1
                ins.then_inc(s_link, 1)
                dve.wait_ge(s_link, steps[0])

            def inv_sqrt(n):
                v, y, nh, t = nw[:, 0, 0:n], rstd[:, 0:n], nw[:, 1, 0:n], nw[:, 2, 0:n]
                link(dve.tensor_scalar(t.bitcast(I32), v.bitcast(I32), 1, None, ALU.logical_shift_right))
                link(dve.tensor_scalar(y.bitcast(I32), t.bitcast(I32), -1.0, RSQRT_MAGIC, ALU.mult, ALU.add))
                dve.tensor_scalar(nh, v, -0.5, None, ALU.mult)
                for _ in range(3):
                    link(dve.tensor_tensor(t, y, y, ALU.mult))
                    link(dve.tensor_tensor(t, t, nh, ALU.mult))
                    link(dve.scalar_tensor_tensor(y, t, 1.5, y, ALU.add, ALU.mult))

            dve.wait_ge(s_in[IN_C], 16)
            dve.wait_ge(s_cexp, 1)
            link(dve.scalar_tensor_tensor(cond[:, :], cond[:, :], 1.0, c_sb[:, :], ALU.add, ALU.mult))
            dve.tensor_scalar(cond[:, :], cond[:, :], 0.5, None, ALU.mult).then_inc(s_cond, 1)

            mods = [0]

            def take_mod(b):
                a, z = BATCH[b]
                l = ADA[a][0]
                j0, j1 = ADA[a][1], ADA[z - 1][1] + 1
                dve.wait_ge(s_ada, z)
                ins = dve.tensor_copy(mod[:, l, j0:j1, :], ada_ps[:, j0 * 8:j1 * 8].rearrange("p (j c) -> p j c", c=DC))
                link(ins)
                dve.wait_ge(s_in[IN_G], 16)
                dve.wait_ge(s_in[IN_G + 1], 16)
                if j0 == 0:
                    ins = dve.scalar_tensor_tensor(mscale[:, l, 0], mod[:, l, 1], 1.0, g_sb[:, 0, l], ALU.add, ALU.mult)
                if j1 == 6:
                    if j0 == 0:
                        link(ins)
                    link(dve.scalar_tensor_tensor(mscale[:, l, 1], mod[:, l, 4], 1.0, g_sb[:, 1, l], ALU.add, ALU.mult))
                    ins = dve.tensor_scalar(ghalf[:, l], mod[:, l, 2], 0.5, None, ALU.mult)
                ins.then_inc(s_mod, 1)

            def norm(l, w):
                g = ("MS", l, w)
                full_wait(dve, g)
                dve.tensor_scalar(nw[:, 0, 0:TT], ps(g)[:, 0:TT], 1.0 / D, EPS, ALU.mult, ALU.add).then_inc(s_ms, 1)
                dve.wait_ge(s_ms, 2 * l + w + 1)
                inv_sqrt(TT)
                dve.wait_ge(s_in[IN_CON], 16)
                for t in range(TT):
                    ins = dve.tensor_scalar(diag[:, t, :], ident, rstd[:, t:t + 1], None, ALU.mult)
                ins.then_inc(s_diag, 1)
                g = ("RB", l, w)
                full_wait(dve, g)
                dve.tensor_tensor(hT[:, :, :], xT[:, :, :],
                                  ps(g)[:, 0:T].unsqueeze(1).to_broadcast([P, DC, T]), ALU.mult).then_inc(s_hn, 1)
                if w == 0 and l == 0:
                    take_mod(0)
                dve.wait_ge(s_hn, 2 * l + w + 1)
                dve.wait_ge(s_mod, [[1, 2], [3, 3]][l][w])
                for cc in range(DC):
                    dve.tensor_scalar(hT[:, cc, :], hT[:, cc, :], mscale[:, l, w, cc:cc + 1],
                                      mod[:, l, 3 * w, cc:cc + 1], ALU.mult, ALU.add).then_inc(s_h, 1)

            def qk(l, k, t):
                q = 8 * l + QN.index((k, t))
                b = q % 2
                heads = 2 if k == "kb" else HA
                m = heads * E
                dve.wait_ge(s_z, 10 * l + ZN.index((k, t)) + 1)
                raw = zraw[:, b, 0:m].rearrange("p (h e) -> p h e", e=E)
                o = zq[:, b, 0:m].rearrange("p (h e) -> p h e", e=E)
                t1 = ztmp[:, 0, 0:m].rearrange("p (h e) -> p h e", e=E)
                t2 = ztmp[:, 1, 0:m].rearrange("p (h e) -> p h e", e=E)
                link(dve.tensor_reduce(nw[:, 3, 0:heads], zsq[:, b, 0:m].rearrange("p (h e) -> p h e", e=E), AX.X, ALU.add))
                link(dve.tensor_scalar(nw[:, 0, 0:heads], nw[:, 3, 0:heads], 1.0 / E, EPS, ALU.mult, ALU.add))
                inv_sqrt(heads)
                if q % 8 >= 2:
                    full_wait(dve, ("QT", l) + QN[q % 8 - 2])
                rope_all = k in ("qb", "kb")
                link(dve.tensor_tensor(raw, raw, rstd[:, 0:heads].unsqueeze(2).to_broadcast([P, heads, E]), ALU.mult))
                dve.wait_ge(s_in[IN_QK + {"qa": 0, "ka": 1, "qb": 2, "kb": 3}[k]], 16)
                gain = qk_gain[:, {"qa": 0, "ka": 1, "qb": 2, "kb": 3}[k], l, :].unsqueeze(1).to_broadcast([P, heads, E])
                if not rope_all:
                    link(dve.tensor_tensor(o, raw, gain, ALU.mult))
                    cos = con[:, C_COSA + t * 16:C_COSA + (t + 1) * 16].unsqueeze(1).to_broadcast([P, heads, 16])
                    sl = con[:, C_SINA + t * 16:C_SINA + t * 16 + 8].unsqueeze(1).to_broadcast([P, heads, 8])
                    sh = con[:, C_SINA + t * 16 + 8:C_SINA + t * 16 + 16].unsqueeze(1).to_broadcast([P, heads, 8])
                    dve.tensor_tensor(t1[:, :, 0:16], o[:, :, 0:16], cos, ALU.mult)
                    dve.tensor_tensor(t2[:, :, 0:8], o[:, :, 8:16], sl, ALU.mult)
                    link(dve.tensor_tensor(t2[:, :, 8:16], o[:, :, 0:8], sh, ALU.mult))
                    dve.tensor_tensor(o[:, :, 0:16], t1[:, :, 0:16], t2[:, :, 0:16], ALU.add).then_inc(s_zq, 1)
                else:
                    link(dve.tensor_tensor(raw, raw, gain, ALU.mult))
                    cos = con[:, C_COSB + t * E:C_COSB + (t + 1) * E].unsqueeze(1).to_broadcast([P, heads, E])
                    dve.tensor_tensor(t1, raw, cos, ALU.mult)
                    for a in range(2):
                        c0 = C_SINB + t * E + a * 32
                        for half in range(2):
                            s = con[:, c0 + half * 16:c0 + half * 16 + 16].unsqueeze(1).to_broadcast([P, heads, 16])
                            lo, hi = a * 32 + half * 16, a * 32 + (1 - half) * 16
                            ins = dve.tensor_tensor(t2[:, :, lo:lo + 16], raw[:, :, hi:hi + 16], s, ALU.mult)
                    link(ins)
                    if k == "qb":
                        dve.tensor_tensor(o, t1, t2, ALU.add).then_inc(s_zq, 1)
                    else:
                        o2 = zq[:, b, 0:2 * m].rearrange("p (h d e) -> p h d e", d=2, e=E)
                        dve.tensor_tensor(o2[:, :, 0, :], t1, t2, ALU.add)
                        dve.tensor_tensor(o2[:, :, 1, :], t1, t2, ALU.add).then_inc(s_zq, 1)

            def head_max(l, h):
                n = NH * l + h
                b = h % 2
                g = ("S", l, h)
                full_wait(dve, g)
                if h >= 2:
                    dve.wait_ge(s_exp, n - 1)
                if h < HA:
                    for t in range(TT):
                        ins = dve.tensor_tensor_reduce(
                            out=sm[:, b, t, :], in0=ps(g)[:, t * T:(t + 1) * T],
                            in1=con[:, C_MASK + t * T:C_MASK + (t + 1) * T], scale=1.0, scalar=-3e38,
                            op0=ALU.add, op1=ALU.max, accum_out=mx[:, b, t:t + 1])
                    link(ins)
                else:
                    link(dve.tensor_reduce(mx[:, b, :], ps(g)[:, :].rearrange("p (t s) -> p t s", t=TT), AX.X, ALU.max))
                dve.tensor_scalar(nmax[:, b, :], mx[:, b, :], -QSCALE, None, ALU.mult).then_inc(s_nm, 1)

            def pT_out(l, h):
                g = ("PT", l, h)
                full_wait(dve, g)
                if h >= 2 and (h - 2) % 4 == 3:
                    full_wait(dve, ("O", l, (h - 2) // 4))
                elif h >= 2:
                    dve.wait_ge(s_pv, 12 * l + 3 * ((h - 2) // 4) + (h - 2) % 4 + 1)
                dve.tensor_copy(pT[:, h % 2], ps(g)[:, :].rearrange("p (s t) -> p s t", s=TT)).then_inc(s_pT, 1)

            def quad_out(l, q):
                g = ("O", l, q)
                br = q // 2
                dve.wait_ge(s_exp, NH * l + 4 * q + 4)
                link(dve.reciprocal(rden[:, q % 2], den[:, q % 2]))
                full_wait(dve, g)
                for t in range(TT):
                    ins = dve.tensor_tensor(
                        ybr[:, br, t, (q % 2) * 256:(q % 2) * 256 + 256].rearrange("p (h e) -> p h e", e=E),
                        ps(g)[:, t * 256:(t + 1) * 256].rearrange("p (h e) -> p h e", e=E),
                        rden[:, q % 2, t].unsqueeze(2).to_broadcast([P, 4, E]), ALU.mult)
                ins.then_inc(s_y, 1)

            def merge(l):
                for q in range(4):
                    g = ("PA", l, q)
                    full_wait(dve, g)
                    if q == 0:
                        dve.wait_ge(s_g, 8 * (l + 1))
                    a = gth[:, 0, 2 * q:2 * q + 2, :]
                    dve.scalar_tensor_tensor(a, a, 1.0, ps(g)[:, :].rearrange("p (c t) -> p c t", c=2),
                                             ALU.add, ALU.mult).then_inc(s_ma, 1)
                for q in range(4):
                    g = ("PB", l, q)
                    full_wait(dve, g)
                    a, b = gth[:, 0, 2 * q:2 * q + 2, :], gth[:, 1, 2 * q:2 * q + 2, :]
                    dve.scalar_tensor_tensor(b, b, 1.0, ps(g)[:, :].rearrange("p (c t) -> p c t", c=2),
                                             ALU.add, ALU.mult).then_inc(s_mb, 1)
                    dve.wait_ge(s_mb, 4 * l + q + 1)
                    dve.wait_ge(s_ma, 4 * l + q + 1)
                    dve.tensor_tensor(a, a, b, ALU.add).then_inc(s_m, 1)

            def residual(l, name, gate, s):
                for cc in range(DC):
                    g = (name, l, cc // 2)
                    full_wait(dve, g)
                    dve.scalar_tensor_tensor(xT[:, cc, :], ps(g)[:, (cc % 2) * T:(cc % 2 + 1) * T], gate[:, cc:cc + 1],
                                             xT[:, cc, :], ALU.mult, ALU.add).then_inc(s, 1)

            def route(l):
                g = ("RT", l)
                prob = rt[:, 0, :]
                tg = lambda r: rt[:, r, :].rearrange("p (g j) -> p g j", j=EG)
                col = lambda r: rt[:, r, 0:TT * NG]
                bc = lambda r: col(r).unsqueeze(2).to_broadcast([P, TT * NG, EG])
                grp = lambda r: col(r).rearrange("p (t g) -> p t g", t=TT)
                full_wait(dve, g)
                link(dve.tensor_reduce(rt[:, 3, 0:TT], ps(g)[:, 0:TT * NE].rearrange("p (t e) -> p t e", t=TT), AX.X, ALU.max))
                dve.tensor_scalar(rt[:, 1, 0:TT], rt[:, 3, 0:TT], -1.0, None, ALU.mult).then_inc(s_rmax, 1)
                dve.wait_ge(s_rexp, l + 1)
                link(dve.reciprocal(rt[:, 3, 0:TT], rt[:, 2, 0:TT]))
                link(dve.tensor_tensor(prob.rearrange("p (t e) -> p t e", t=TT), prob.rearrange("p (t e) -> p t e", t=TT),
                                       rt[:, 3, 0:TT].unsqueeze(2).to_broadcast([P, TT, NE]), ALU.mult))
                d = desc.unsqueeze(1).to_broadcast([P, TT * NG, EG])

                def first_max(src, best, onehot):
                    link(dve.tensor_reduce(col(best), tg(src), AX.X, ALU.max))
                    link(dve.tensor_tensor(tg(4), tg(src), bc(best), ALU.is_equal))
                    link(dve.tensor_tensor(tg(4), tg(4), d, ALU.mult))
                    link(dve.tensor_reduce(col(5), tg(4), AX.X, ALU.max))
                    link(dve.tensor_tensor(tg(onehot), tg(4), bc(5), ALU.is_equal))

                first_max(0, 6, 8)
                link(dve.scalar_tensor_tensor(rt[:, 7, :], rt[:, 8, :], -4.0, rt[:, 0, :], ALU.mult, ALU.add))
                first_max(7, 9, 10)
                link(dve.tensor_tensor(col(11), col(6), col(9), ALU.add))
                link(dve.tensor_reduce(rt[:, 12, 0:TT], grp(11), AX.X, ALU.max))
                link(dve.tensor_tensor(grp(13), grp(11), rt[:, 12, 0:TT].unsqueeze(2).to_broadcast([P, TT, NG]), ALU.is_equal))
                link(dve.tensor_tensor(grp(13), grp(13), desc[:, 0:NG].unsqueeze(1).to_broadcast([P, TT, NG]), ALU.mult))
                link(dve.tensor_reduce(rt[:, 12, 0:TT], grp(13), AX.X, ALU.max))
                link(dve.tensor_tensor(grp(14), grp(13), rt[:, 12, 0:TT].unsqueeze(2).to_broadcast([P, TT, NG]), ALU.is_equal))
                link(dve.tensor_tensor(tg(8), tg(8), bc(14), ALU.mult))
                link(dve.tensor_tensor(tg(10), tg(10), bc(14), ALU.mult))
                dve.tensor_tensor(rt[:, 15, :], rt[:, 8, :], rt[:, 10, :], ALU.add).then_inc(s_sel, 1)
                link(dve.reciprocal(col(16), col(11)))
                link(dve.tensor_tensor(col(16), col(16), col(14), ALU.mult))
                dve.tensor_tensor(col(17), col(16), col(6), ALU.mult)
                link(dve.tensor_tensor(col(18), col(16), col(9), ALU.mult))
                dve.tensor_reduce(rt[:, 19, 0:TT], grp(17), AX.X, ALU.add)
                link(dve.tensor_reduce(rt[:, 20, 0:TT], grp(18), AX.X, ALU.add))
                full_wait(dve, ("CNT", l))
                dve.tensor_copy(ccol[:, :], ps(("CNT", l))[0:NE, 0:P]).then_inc(s_cnt, 1)
                full_wait(dve, ("START", l))
                st = ps(("START", l))
                link(dve.tensor_reduce(rt[0:1, 21, 0:1], st[0:1, NE:2 * NE], AX.X, ALU.max))
                link(dve.tensor_copy(tables[l][0:1, NBLK * NE:NBLK * NE + 1], rt[0:1, 21, 0:1]))
                link(dve.tensor_copy(rt[:, 22, 0:NE], st[:, 0:NE]))
                for b in range(NBLK):
                    ins = dve.tensor_scalar(tables[l][0:1, b * NE:(b + 1) * NE], rt[0:1, 22, 0:NE], float(b * W), float(SLOTS),
                                            ALU.add, ALU.min)
                ins.then_inc(s_tab, 1)
                full_wait(dve, ("POS", l))
                p2 = lambda r: rt[:, r, :].rearrange("p (t e) -> p t e", t=TT)
                dve.tensor_tensor(p2(23), ps(("POS", l))[:, 0:TT * NE].rearrange("p (t e) -> p t e", t=TT),
                                  rt[:, 22, 0:NE].unsqueeze(1).to_broadcast([P, TT, NE]), ALU.add).then_inc(s_slot, 1)
                dve.wait_ge(s_slot, l + 1)
                dve.tensor_tensor(rt[:, 4, :], rt[:, 8, :], rt[:, 23, :], ALU.mult)
                link(dve.tensor_tensor(rt[:, 7, :], rt[:, 10, :], rt[:, 23, :], ALU.mult))
                dve.tensor_reduce(rt[:, 5, 0:TT], p2(4), AX.X, ALU.add)
                link(dve.tensor_reduce(rt[:, 6, 0:TT], p2(7), AX.X, ALU.add))
                for t in range(TT):
                    dve.tensor_scalar(sel_t[:, t], iota, rt[:, 5, t:t + 1], None, ALU.is_equal)
                    dve.tensor_scalar(sel_w[:, t], iota, rt[:, 6, t:t + 1], None, ALU.is_equal)
                    steps_before = steps[0]
                    link(dve.tensor_scalar(nw[:, 3, 0:TT], rt[:, 5, 0:TT], 0.0, None, ALU.mult))
                    assert steps[0] == steps_before + 1
                    dve.tensor_tensor(sel_s[:, t], sel_t[:, t], sel_w[:, t], ALU.add).then_inc(s_S, 1)
                dve.wait_ge(s_S, TT * (l + 1))
                for t in range(TT):
                    link(dve.tensor_scalar(sel_w[:, t], sel_w[:, t], rt[:, 20, t:t + 1], None, ALU.mult))
                    dve.scalar_tensor_tensor(sel_w[:, t], sel_t[:, t], rt[:, 19, t:t + 1], sel_w[:, t],
                                             ALU.mult, ALU.add).then_inc(s_Wm, 1)

            def swish(e, j, l, steady):
                g = bank[3 * j][:, 0:FC * W].rearrange("p (f s) -> p f s", f=FC)
                u = bank[3 * j + 1][:, 0:FC * W].rearrange("p (f s) -> p f s", f=FC)
                dve.wait_ge(s_th, e + (NE * l + 1))
                dve.scalar_tensor_tensor(sw[:, j], th[:, j], 1.0, g, ALU.add, ALU.mult).then_inc(s_sw, 1)
                dve.wait_ge(s_sw, e + (NE * l + 1))
                dve.wait_ge(s_ud, e + (NE * l + 1))
                if steady:
                    dve.wait_ge(s_yd, e + (NE * l - 1))
                dve.scalar_tensor_tensor(hb[:, j], sw[:, j], 0.5, u, ALU.mult, ALU.mult).then_inc(s_hb, 1)

            for l in range(DEPTH):
                norm(l, 0)
                for k, t in QN:
                    qk(l, k, t)
                for h in range(NH + 1):
                    if h < NH:
                        head_max(l, h)
                    if h >= 1:
                        pT_out(l, h - 1)
                        if (h - 1) % 4 == 3:
                            quad_out(l, (h - 1) // 4)
                    if l == 0 and h == 7:
                        take_mod(1)
                if l == 0:
                    take_mod(2)
                merge(l)
                dve.wait_ge(s_mod, 2 if l == 0 else 3)
                residual(l, "OUT", ghalf[:, l], s_x1)
                norm(l, 1)
                route(l)
                for cc in range(1, DC, 2):
                    g = ("XS", l, cc)
                    full_wait(dve, g)
                    dve.tensor_copy(xs[:, cc, 0:SLOTS], ps(g)[:, :]).then_inc(s_xsv, 1)
                for j in range(2):
                    swish(j, j, l, False)
                with dve.Fori(1, NE // 2) as i:
                    for j in range(2):
                        swish(i * 2 + j, j, l, True)
                count = dve.value_load(tables[l][0:1, NBLK * NE:NBLK * NE + 1], min_val=0, max_val=T)
                with dve.If(count > overflow_at):
                    f = fb[l]
                    g = bank[0][:, 0:FC * W].rearrange("p (f s) -> p f s", f=FC)
                    u = bank[1][:, 0:FC * W].rearrange("p (f s) -> p f s", f=FC)
                    dve.wait_ge(s_yd, NE * (l + 1))
                    with dve.Fori(0, NE) as e:
                        for b in range(NBLK):
                            dve.wait_ge(f["tanh"], e * NBLK + (b + 1))
                            dve.scalar_tensor_tensor(sw[:, 0], th[:, 0], 1.0, g, ALU.add, ALU.mult).then_inc(f["swish"], 1)
                            dve.wait_ge(f["swish"], e * NBLK + (b + 1))
                            dve.scalar_tensor_tensor(hb[:, 0], sw[:, 0], 0.5, u, ALU.mult, ALU.mult).then_inc(f["h"], 1)
                for q in range(1, 8, 2):
                    g = ("YS", l, q)
                    full_wait(dve, g)
                    dve.tensor_copy(yd[:, q // 2, 512:1024], ps(g)[:, :]).then_inc(s_yev, 1)
                residual(l, "CMB", mod[:, l, 5], s_x2)

        @block.tensor
        def _(pe):
            order = iter(psum_groups())

            def begin(g):
                assert next(order) == g, g
                bank_wait(pe, g)

            pe.wait_ge(s_in[IN_X], 16)
            pe.wait_ge(s_in[IN_CON], 16)
            for q in range(4):
                g = ("XT", q)
                begin(g)
                for n in range(4):
                    cc, t = 2 * q + n // 2, n % 2
                    ins = pe.transpose(ps(g)[:, n * P:(n + 1) * P], xin[:, t, cc:D:DC], ident)
                full_inc(ins, g)

            def norm(l, w):
                g = ("MS", l, w)
                begin(g)
                pe.wait_ge(s_sq, 2 * l + w + 1)
                for t in range(TT):
                    for cc in range(DC):
                        ins = pe.matmul(ps(g)[:, t:t + 1], hT[:, cc, t * P:(t + 1) * P], ones[:, 0:1],
                                        start=(cc == 0), stop=(cc == DC - 1))
                full_inc(ins, g)
                g = ("RB", l, w)
                begin(g)
                pe.wait_ge(s_diag, 2 * l + w + 1)
                for t in range(TT):
                    ins = pe.matmul(ps(g)[:, t * P:(t + 1) * P], ones, diag[:, t, :], start=True, stop=True)
                full_inc(ins, g)

            def ada(n):
                l, j, kh = ADA[n]
                for b, (a, z) in enumerate(BATCH):
                    if n == a:
                        j0, j1 = ADA[a][1], ADA[z - 1][1] + 1
                        if b:
                            pe.wait_ge(s_mod, b)
                        pe.wait_ge(s_in[IN_B], 16)
                        pe.wait_ge(s_cond, 1)
                        pe.matmul(ada_ps[:, j0 * 8:j1 * 8], ident, b_sb[:, l, j0:j1, :], start=True, stop=False,
                                  skip_group_check=True)
                weights_wait(pe, ("ada", n))
                wt = ring[:, slot_of(("ada", n)), :].rearrange("p (c n) -> p c n", c=4)
                for cc in range(DC):
                    for k in range(4):
                        ins = pe.matmul(ada_ps[:, j * 8 + cc:j * 8 + cc + 1], wt[:, k, cc:D:DC],
                                        cond[:, 4 * kh + k:4 * kh + k + 1], start=False, stop=True,
                                        skip_group_check=True)
                ins.then_inc(s_ada, 1)

            def z(l, k):
                it = ("z", l, k)
                n = Z_COLS[k][1]
                wt = ring[:, slot_of(it), 0:DC * n].rearrange("p (c n) -> p c n", c=DC)
                for t in range(TT):
                    g = ("Z", l, k, t)
                    begin(g)
                    if t == 0:
                        weights_wait(pe, it)
                    for cc in range(DC):
                        if t == 0 and k == Z_KINDS[0]:
                            pe.wait_ge(s_h, 16 * l + cc + 1)
                        ins = pe.matmul(ps(g)[:, 0:n], hT[:, cc, t * P:(t + 1) * P], wt[:, cc, :],
                                        start=(cc == 0), stop=(cc == DC - 1))
                    full_inc(ins, g)

            def qk_T(l, k, t):
                q = 8 * l + QN.index((k, t))
                g = ("QT", l, k, t)
                begin(g)
                pe.wait_ge(s_zq, q + 1)
                for n in range(2 if k == "kb" else 4):
                    ins = pe.transpose(ps(g)[:, n * P:(n + 1) * P], zq[:, q % 2, n * P:(n + 1) * P], ident)
                full_inc(ins, g)

            def scores(l, h):
                g = ("S", l, h)
                begin(g)
                half = 64 * (h % 2)
                if h < HA:
                    pe.wait_ge(s_qT, 8 * l + 4)
                    q, k = qT["qa"][half:half + 64, h // 2], qT["ka"][half:half + 64, h // 2]
                else:
                    pe.wait_ge(s_qT, 8 * l + 8)
                    q, k = qT["qb"][half:half + 64, (h - HA) // 2], qT["kb"][half:half + 64, (h - HA) // 4]
                for t in range(TT):
                    ins = pe.matmul(ps(g)[:, t * T:(t + 1) * T], q[:, t * P:(t + 1) * P], k, start=True, stop=True)
                full_inc(ins, g)

            def probs_T(l, h):
                g = ("PT", l, h)
                begin(g)
                pe.wait_ge(s_exp, NH * l + h + 1)
                for s in range(TT):
                    for t in range(TT):
                        ins = pe.transpose(ps(g)[:, (s * TT + t) * P:(s * TT + t + 1) * P],
                                           pr[:, h % 2, t, s * P:(s + 1) * P], ident)
                full_inc(ins, g)

            def values(l, h):
                g = ("O", l, h // 4)
                if h % 4 == 0:
                    begin(g)
                if h == 0:
                    pe.wait_ge(s_z, 10 * l + ZN.index(("va", TT - 1)) + 1)
                if h == HA:
                    pe.wait_ge(s_z, 10 * l + ZN.index(("kb", TT - 1)) + 1)
                pe.wait_ge(s_pT, NH * l + h + 1)
                for t in range(TT):
                    o = ps(g)[:, t * 256 + (h % 4) * E:t * 256 + (h % 4 + 1) * E]
                    for s in range(TT):
                        v = va[:, s, h * E:(h + 1) * E] if h < HA else vb[:, s, (h - HA) // 4 * E:((h - HA) // 4 + 1) * E]
                        ins = pe.matmul(o, pT[:, h % 2, s, t * P:(t + 1) * P], v, start=(s == 0), stop=(s == TT - 1))
                if h % 4 == 3:
                    full_inc(ins, g)
                else:
                    ins.then_inc(s_pv, 1)

            def branch_T(l, q):
                g = ("YT", l, q)
                begin(g)
                pe.wait_ge(s_y, 4 * l + q + 1)
                for n in range(4):
                    pair, t = divmod(n, TT)
                    a = (q % 2) * 256 + pair * P
                    ins = pe.transpose(ps(g)[:, n * P:(n + 1) * P], ybr[:, q // 2, t, a:a + P], ident)
                full_inc(ins, g)

            def gate(l, m):
                it = ("gate", l, m // 4)
                wt = ring[:, slot_of(it), :].rearrange("p (c n) -> p c n", c=DC)
                g = ("G", l, m // 2)
                if m % 2 == 0:
                    begin(g)
                if m % 4 == 0:
                    weights_wait(pe, it)
                for cc in range(DC):
                    ins = pe.matmul(ps(g)[:, (m % 2) * T:(m % 2 + 1) * T], wt[:, cc, (m % 4) * P:(m % 4 + 1) * P],
                                    hT[:, cc, :], start=(cc == 0), stop=(cc == DC - 1))
                if m % 2:
                    full_inc(ins, g)

            def project(l, name, it, br):
                wt = ring[:, slot_of(it), :].rearrange("p (c n) -> p c n", c=4)
                for q in range(4):
                    g = (name, l, q)
                    begin(g)
                    if q == 0:
                        weights_wait(pe, it)
                        pe.wait_ge(s_yT, 4 * l + 2 * br + 2)
                    for u in range(2):
                        m = 2 * q + u
                        for k in range(4):
                            ins = pe.matmul(ps(g)[:, u * T:(u + 1) * T], wt[:, k, m * P:(m + 1) * P], yT[:, br, k, :],
                                            start=(k == 0), stop=(k == 3))
                    full_inc(ins, g)

            def project_out(l):
                for half in range(2):
                    it = ("out", l, half)
                    weights_wait(pe, it)
                    wt = ring[:, slot_of(it), :].rearrange("p (c n) -> p c n", c=4)
                    for q in range(4):
                        g = ("OUT", l, q)
                        if half == 0:
                            begin(g)
                        for u in range(2):
                            cc = 2 * q + u
                            for k in range(4):
                                if q == 0 and u == 0 and k % 2 == 0:
                                    pe.wait_ge(s_m, 4 * l + (4 * half + k) // 2 + 1)
                                ins = pe.matmul(ps(g)[:, u * T:(u + 1) * T], wt[:, k, cc:D:DC], gth[:, 0, 4 * half + k, :],
                                                start=(half == 0 and u == 0 and k == 0), stop=(half == 1 and k == 3),
                                                skip_group_check=True)
                        if half == 1:
                            full_inc(ins, g)
                    if half == 0:
                        ins.then_inc(s_out0, 1)

            def route(l):
                g = ("RT", l)
                begin(g)
                pe.wait_ge(s_in[IN_WR], 16)
                pe.wait_ge(s_h, 16 * l + 16)
                for t in range(TT):
                    for cc in range(DC):
                        ins = pe.matmul(ps(g)[:, t * NE:(t + 1) * NE], hT[:, cc, t * P:(t + 1) * P], wr_sb[:, cc, :],
                                        start=(cc == 0), stop=(cc == DC - 1))
                full_inc(ins, g)
                for q in range(4):
                    g = ("H2", l, q)
                    begin(g)
                    for n in range(4):
                        t, cc = q // 2, 4 * (q % 2) + n
                        ins = pe.transpose(ps(g)[:, n * P:(n + 1) * P], hT[:, cc, t * P:(t + 1) * P], ident)
                    full_inc(ins, g)
                sel = rt[:, 15, :]
                g = ("CNT", l)
                begin(g)
                pe.wait_ge(s_sel, l + 1)
                for t in range(TT):
                    ins = pe.matmul(ps(g)[0:NE, 0:P], sel[:, t * NE:(t + 1) * NE], ones, start=(t == 0), stop=(t == TT - 1))
                full_inc(ins, g)
                g = ("START", l)
                begin(g)
                for t in range(TT):
                    pe.matmul(ps(g)[:, NE:2 * NE], ones, sel[:, t * NE:(t + 1) * NE], start=(t == 0), stop=(t == TT - 1))
                pe.wait_ge(s_cnt, l + 1)
                ins = pe.matmul(ps(g)[:, 0:NE], ccol[:, :], upper[0:NE, 0:NE], start=True, stop=True)
                full_inc(ins, g)
                g = ("POS", l)
                begin(g)
                pe.matmul(ps(g)[:, 0:NE], upper, sel[:, 0:NE], start=True, stop=True)
                pe.matmul(ps(g)[:, NE:2 * NE], ones, sel[:, 0:NE], start=True, stop=False)
                ins = pe.matmul(ps(g)[:, NE:2 * NE], upper, sel[:, NE:2 * NE], start=False, stop=True)
                full_inc(ins, g)
                for cc in range(DC):
                    g = ("XS", l, cc)
                    begin(g)
                    if cc == 0:
                        pe.wait_ge(s_h2, 4 * l + 4)
                    for t in range(TT):
                        if cc == 0:
                            pe.wait_ge(s_S, TT * l + t + 1)
                        ins = pe.matmul(ps(g)[:, :], h2[:, t, cc, :], sel_s[:, t], start=(t == 0), stop=(t == TT - 1))
                    full_inc(ins, g)
                for q in range(2):
                    g = ("WT", l, q)
                    begin(g)
                    if q == 0:
                        pe.wait_ge(s_Wm, TT * (l + 1))
                    for n in range(4):
                        s, t = 2 * q + n // TT, n % TT
                        ins = pe.transpose(ps(g)[:, n * P:(n + 1) * P], sel_w[:, t, s * P:(s + 1) * P], ident)
                    full_inc(ins, g)

            def gate_up(wt, dst, xb, s):
                wv = wt.rearrange("p (c n) -> p c n", c=DC)
                for m in range(FC):
                    for cc in range(DC):
                        ins = pe.matmul(dst[:, m * W:(m + 1) * W], wv[:, cc, m * P:(m + 1) * P], xb[:, cc, :],
                                        start=(cc == 0), stop=(cc == DC - 1))
                ins.then_inc(s, 1)

            def down(wt, dst, hid, s):
                wv = wt.rearrange("p (c n) -> p c n", c=FC)
                for cc in range(DC):
                    for m in range(FC):
                        ins = pe.matmul(dst[:, cc * W:(cc + 1) * W], wv[:, m, cc * P:(cc + 1) * P], hid[:, m, :],
                                        start=(m == 0), stop=(m == FC - 1))
                ins.then_inc(s, 1)

            def expert(l, i, j, steady):
                e = i * 2 + j
                n = index[("wg", l, 0)] + 3 * j
                lw = lambda k: pe.wait_ge(landed[(n + k) % RING], i * 16 + 16 * ((n + k) // RING + 1))
                pe.wait_ge(s_xb, e + (NE * l + 1))
                lw(0)
                gate_up(ring[:, n % RING, :], bank[3 * j], xblk[:, j], s_gd)
                lw(1)
                gate_up(ring[:, (n + 1) % RING, :], bank[3 * j + 1], xblk[:, j], s_ud)
                if steady:
                    pe.wait_ge(s_ys, e + (NE * l - 1))
                pe.wait_ge(s_hb, e + (NE * l + 1))
                lw(2)
                down(ring[:, (n + 2) % RING, :], bank[3 * j + 2], hb[:, j], s_yd)

            def experts(l):
                begin(("MOE", l))
                for j in range(2):
                    expert(l, 0, j, False)
                with pe.Fori(1, NE // 2) as i:
                    for j in range(2):
                        expert(l, i, j, True)
                count = pe.value_load(tables[l][0:1, NBLK * NE:NBLK * NE + 1], min_val=0, max_val=T)
                with pe.If(count > overflow_at):
                    f = fb[l]
                    pe.wait_ge(s_ys, NE * (l + 1))
                    pe.wait_ge(s_yd, NE * (l + 1))
                    pe.sem_inc(f["down"], 1)
                    pe.sem_inc(f["up"], 1)
                    with pe.Fori(0, NE) as e:
                        pe.wait_ge(f["landed"], e * 48 + 48)
                        for b in range(NBLK):
                            pe.wait_ge(f["x"], e * NBLK + (b + 1))
                            gate_up2(f)
                            pe.wait_ge(f["h"], e * NBLK + (b + 1))
                            pe.wait_ge(f["ys"], e * NBLK + (b + 1))
                            down(ring[:, 2, :], bank[2], hb[:, 0], f["down"])
                    pe.wait_ge(f["ys"], NE * NBLK + 1)

            def gate_up2(f):
                wv = ring[:, 0:2, :].rearrange("p w (c n) -> p w c n", c=DC)
                for w in range(2):
                    for m in range(FC):
                        for cc in range(DC):
                            ins = pe.matmul(bank[w][:, m * W:(m + 1) * W], wv[:, w, cc, m * P:(m + 1) * P],
                                            xblk[:, 0, cc, :], start=(cc == 0), stop=(cc == DC - 1))
                ins.then_inc(f["up"], 1)

            def combine(l):
                for q in range(8):
                    g = ("YS", l, q)
                    begin(g)
                    if q == 0:
                        pe.wait_ge(s_ys, NE * (l + 1))
                    for n in range(4):
                        s, cc = q // 2, 4 * (q % 2) + n
                        ins = pe.transpose(ps(g)[:, n * P:(n + 1) * P], ys[:, cc, s * P:(s + 1) * P], ident)
                    full_inc(ins, g)
                for q in range(4):
                    g = ("CMB", l, q)
                    begin(g)
                    if q == 0:
                        pe.wait_ge(s_yea, 4 * (l + 1))
                        pe.wait_ge(s_yev, 4 * (l + 1))
                        pe.wait_ge(s_wT, 2 * (l + 1))
                    for u in range(2):
                        for s in range(4):
                            ins = pe.matmul(ps(g)[:, u * T:(u + 1) * T], yd[:, s, 2 * q + u:D:DC], wT[:, s, :],
                                            start=(s == 0), stop=(s == 3))
                    full_inc(ins, g)

            norm(0, 0)
            for n in range(4):
                ada(n)
            for l in range(DEPTH):
                if l:
                    norm(l, 0)
                for n, k in enumerate(Z_KINDS):
                    z(l, k)
                    if n:
                        for t in range(TT):
                            qk_T(l, Z_KINDS[n - 1], t)
                for h in range(NH + 1):
                    if h < NH:
                        scores(l, h)
                    if h >= 1:
                        probs_T(l, h - 1)
                    if h < NH:
                        for f in filler(l, h):
                            if f[0] == "gate":
                                gate(l, f[1])
                            else:
                                ada(f[1])
                    if h >= 1:
                        values(l, h - 1)
                        if (h - 1) % 4 == 3:
                            branch_T(l, (h - 1) // 4)
                project(l, "PA", ("pa", l), 0)
                project(l, "PB", ("pb", l), 1)
                project_out(l)
                norm(l, 1)
                route(l)
                experts(l)
                combine(l)
            for q in range(4):
                g = ("FIN", q)
                begin(g)
                if q == 0:
                    pe.wait_ge(s_x2, 8 * DEPTH)
                for n in range(4):
                    ins = pe.transpose(ps(g)[:, n * P:(n + 1) * P],
                                       xT[:, 4 * (q % 2) + n, (q // 2) * P:(q // 2 + 1) * P], ident)
                full_inc(ins, g)


_INS = ["x", "c", "w_ada", "b_ada", "g_mix", "w_in", "qn_a", "kn_a", "qn_b", "kn_b", "w_pa", "w_pb", "w_out",
        "g_ffn", "w_router", "w_gate", "w_up", "w_down"]


def kernel(**inputs):
    import concourse.bacc as _bacc
    from concourse.bass_utils import run_bass_kernel_spmd as _run

    nc = _bacc.Bacc("TRN2", target_bir_lowering=False, num_devices=1)
    arrays, args = {}, []
    given = [(name, np.ascontiguousarray(inputs[name])) for name in _INS] + [("const", constants())]
    for name, a in given:
        arrays[f"in_{name}_dram"] = a
        args.append(nc.dram_tensor(f"in_{name}_dram", a.shape, mybir.dt.from_np(a.dtype), kind="ExternalInput").ap())
    args.append(nc.dram_tensor("out_0_dram", (1, T, D), F32, kind="ExternalOutput").ap())
    build(nc, *args)
    r = _run(nc, [arrays], core_ids=[0])
    return r.results[0]["out_0_dram"]
```

```python
from contextlib import ExitStack

import numpy as np

import concourse.bass as bass
from concourse import mybir

ALU = mybir.AluOpType
ACT = mybir.ActivationFunctionType
AX = mybir.AxisListType
F32 = mybir.dt.float32
I32 = mybir.dt.int32

P = 128
D = 1024
T = 256
DEPTH = 2
DC = D // P
TT = T // P
E = 64
HA = 8
KVB = 2
NH = 2 * HA
AW = HA * E
IN_COLS = 3 * AW + AW + 2 * KVB * E + 2 * D
NE = 32
NG = 4
EG = NE // NG
FF = D // 2
FC = FF // P
W = 64
NBLK = T // W
SLOTS = 2 * T
SPAD = SLOTS + W
EPS = 1e-6
QSCALE = E ** -0.5
MASKED = -1e37
RSQRT_MAGIC = 1597463007.0

SCRATCH = 512
RING = 6
RW = 4096

C_ID, C_ONE, C_UP, C_MASK = 0, 128, 256, 384
C_COSA, C_SINA = 896, 928
C_COSB, C_SINB = 960, 1088
C_IOTA, C_DESC = 1216, 1728
NCONST = 1736


def constants():
    k = np.zeros((P, NCONST), np.float32)
    k[:, C_ID:C_ID + P] = np.eye(P)
    k[:, C_ONE:C_ONE + P] = 1.0
    k[:, C_UP:C_UP + P] = np.triu(np.ones((P, P)), 1)
    t = np.arange(T)
    gap = np.abs(t[:, None] - t[None, :])
    count = (gap <= 64).astype(int) + (gap % 4 == 0) + (gap % 16 == 0)
    mask = np.where(count > 0, np.log(np.maximum(count, 1)) / QSCALE, MASKED)

    def rotary(pos, half, theta):
        freq = np.float32(theta) ** (-np.arange(half, dtype=np.float32) / np.float32(half))
        ang = (pos.astype(np.float32)[:, None] * freq.astype(np.float32)).astype(np.float32).astype(np.float64)
        cos, sin = np.cos(ang), np.sin(ang)
        return np.concatenate([cos, cos], 1), np.concatenate([-sin, sin], 1)

    ca, sa = rotary(t, 8, 500000.0)
    cr, sr = rotary(t // 64, 16, 10000.0)
    cc, sc = rotary(t % 64, 16, 10000.0)
    cb, sb = np.concatenate([cr, cc], 1), np.concatenate([sr, sc], 1)
    for n in range(TT):
        rows = slice(n * P, (n + 1) * P)
        k[:, C_MASK + n * T:C_MASK + (n + 1) * T] = mask[rows]
        k[:, C_COSA + n * 16:C_COSA + (n + 1) * 16] = ca[rows]
        k[:, C_SINA + n * 16:C_SINA + (n + 1) * 16] = sa[rows]
        k[:, C_COSB + n * E:C_COSB + (n + 1) * E] = cb[rows]
        k[:, C_SINB + n * E:C_SINB + (n + 1) * E] = sb[rows]
    k[:, C_IOTA:C_IOTA + SLOTS] = np.arange(SLOTS)
    k[:, C_DESC:C_DESC + EG] = EG - np.arange(EG)
    return k


ADA = [(l, jp, cp) for l in range(DEPTH) for jp in range(3) for cp in range(4)]
Z_KINDS = ["qa", "ka", "kb", "qb", "va"]
ZN = [(k, t) for k in Z_KINDS for t in range(TT)]
QN = [(k, t) for k in ("qa", "ka", "kb", "qb") for t in range(TT)]
ADA_BATCHES = len(ADA) // 4
Z_COLS = {"qa": (0, 512), "ka": (512, 512), "va": (1024, 512), "qb": (1536, 512), "kb": (2048, 256)}
GATE_COL = IN_COLS - 2 * D


AFTER_Z = {0: range(4, 8), 1: range(16, 20)}
IN_HEADS = {0: range(8, 16), 1: range(20, 24)}
BATCHES = {0: range(1, 4), 1: range(4, 6)}


def z_filler(l, n):
    return [AFTER_Z[l][n - 1]] if n else []


def filler(l, h):
    return [("gate", h)] + ([("ada", IN_HEADS[l][h // 2])] if h % 2 and h // 2 < len(IN_HEADS[l]) else [])


def weight_items():
    items = [("ada", n) for n in range(4)]
    for l in range(DEPTH):
        for n, k in enumerate(Z_KINDS):
            items += [("z", l, k)] + [("ada", a) for a in z_filler(l, n)]
        for h in range(NH):
            for f in filler(l, h):
                if f[0] == "ada":
                    items.append(f)
                elif f[1] % 4 == 0:
                    items.append(("gate", l, f[1] // 4))
        items += [("pa", l), ("pb", l), ("out", l, 0), ("out", l, 1)]
        for e in range(NE + 1):
            items += [(w, l, e) for w in ("wg", "wu") if e < NE and e != 2]
            items += [("wd", l, e - 1)] if e else []
    return items


def rows_taken(l, h):
    if h < 0:
        return [BATCHES[l][0]]
    return [f[1] // 4 for f in filler(l, h) if f[0] == "ada" and f[1] % 4 == 3]


def psum_groups():
    g = [("XT", q) for q in range(4)]
    for l in range(DEPTH):
        g += [("MS", l, 0), ("RB", l, 0)]
        if l == 0:
            g.append(("AC",))
        for n, k in enumerate(Z_KINDS):
            g += [("Z", l, k, t) for t in range(TT)]
            if n:
                g += [("QT", l, Z_KINDS[n - 1], t) for t in range(TT)]
        for h in range(NH + 1):
            if h < NH:
                g.append(("S", l, h))
            if h >= 1:
                g.append(("PT", l, h - 1))
            if h < NH:
                for f in filler(l, h):
                    if f[0] == "gate" and f[1] % 2 == 0:
                        g.append(("G", l, f[1] // 2))
            if h >= 2 and (h - 2) % 4 == 0:
                g.append(("O", l, (h - 2) // 4))
        for n in ("PA", "PB", "OUT"):
            g += [(n, l, q) for q in range(4)]
        g += [("MS", l, 1), ("RB", l, 1)]
        g += [("RT", l)] + [("H2", l, q) for q in range(4)]
        g += [("CNT", l), ("START", l), ("POS", l)]
        g += [("XS", l, c) for c in range(DC)] + [("WT", l, q) for q in range(2)]
        g += [("MOE", l)]
        g += [("YS", l, q) for q in range(8)] + [("CMB", l, q) for q in range(4)]
    g += [("FIN", q) for q in range(4)]
    return g


NBANK = 7


def plan_banks():
    place, before, owner, full = {}, {}, [None] * NBANK, [0] * NBANK
    n = 0
    for g in psum_groups():
        if g[0] == "MOE":
            before[g] = [o for o in owner if o is not None]
            for b in range(NBANK):
                owner[b] = g
            n = 0
            continue
        if g[0] == "O":
            b = NBANK - 1
        else:
            b = n % (NBANK - 1)
            n += 1
        before[g] = [owner[b]] if owner[b] is not None else []
        full[b] += 1
        place[g] = (b, full[b])
        owner[b] = g
    return place, before


def build(nc, x, c, w_ada, b_ada, g_mix, w_in, qn_a, kn_a, qn_b, kn_b, w_pa, w_pb, w_out, g_ffn,
          w_router, w_gate, w_up, w_down, const, out, overflow_at=W):
    place, before = plan_banks()
    items = weight_items()
    index = {it: n for n, it in enumerate(items)}

    ctx = ExitStack()
    with ctx:
        def sb(name, shape, dt=F32):
            return ctx.enter_context(nc.sbuf_tensor(name, shape, dt))

        def sem(name):
            return ctx.enter_context(nc.semaphore(name))

        ring = sb("ring", [P, RING, RW])
        third_up = sb("third_up", [P, RW])
        xT = sb("xT", [P, DC, T])
        hT = sb("hT", [P, DC, T])
        con = sb("con", [P, NCONST])
        g_sb = sb("g_sb", [P, 2, DEPTH, DC])
        qk_gain = sb("qk_gain", [P, 4, DEPTH, E])
        b_sb = sb("b_sb", [P, DEPTH, 6, DC])
        wr_sb = sb("wr_sb", [P, DC + 3, NE])
        c_sb = sb("c_sb", [P, DC])
        cond = sb("cond", [P, DC])
        cond32 = sb("cond32", [P, DC, 32])
        adarow = sb("adarow", [P, 512])
        modraw = sb("modraw", [P, DEPTH, 6, DC])
        mod = sb("mod", [P, DEPTH, 6, DC])
        mscale = sb("mscale", [P, DEPTH, 2, DC])
        ghalf = sb("ghalf", [P, DEPTH, DC])
        nw = sb("nw", [P, 4, 8])
        rstd = sb("rstd", [P, 8])
        diag = sb("diag", [P, TT, P])
        ccol = sb("ccol", [NE, P])
        tables = [sb(f"table{l}", [1, NBLK * NE + 1], I32) for l in range(DEPTH)]
        mx = sb("mx", [P, 2, TT])
        nmax = sb("nmax", [P, 2, TT])
        den = sb("den", [P, 2, TT])
        rden = sb("rden", [P, 2, TT])

        WORK = 19712
        work = sb("work", [P, WORK])
        at = [0]

        def part(n):
            a = work[:, at[0]:at[0] + n]
            at[0] += n
            assert at[0] <= WORK
            return a

        va = part(TT * AW).rearrange("p (t n) -> p t n", t=TT)
        vb = part(TT * KVB * E).rearrange("p (t n) -> p t n", t=TT)
        qT = {k: part(4 * T).rearrange("p (c t) -> p c t", c=4) for k in ("qa", "qb")}
        kz = part(12 * T).rearrange("p (c u t) -> p c u t", c=6, u=2)
        kT = {"ka": kz[:, 0:4], "kb": kz[:, 4:6]}
        zsq = part(2 * AW).rearrange("p (b n) -> p b n", b=2)
        zraw = part(2 * AW).rearrange("p (b n) -> p b n", b=2)
        zq = part(2 * AW).rearrange("p (b n) -> p b n", b=2)
        ztmp = part(2 * AW).rearrange("p (b n) -> p b n", b=2)
        gth = part(2 * DC * T).rearrange("p (b c t) -> p b c t", b=2, c=DC)
        yT = part(2 * 4 * T).rearrange("p (b c t) -> p b c t", b=2, c=4)
        sm = part(2 * TT * T).rearrange("p (b t n) -> p b t n", b=2, t=TT)
        pr = part(2 * TT * T).rearrange("p (b t n) -> p b t n", b=2, t=TT)
        pT = part(2 * TT * T).rearrange("p (b t n) -> p b t n", b=2, t=TT)
        third_gate = work[:, 5120:5120 + RW]
        at[0] = 0
        xs = part(DC * SPAD).rearrange("p (c s) -> p c s", c=DC)
        ys = part(DC * SPAD).rearrange("p (c s) -> p c s", c=DC)
        sel_s = part(TT * SLOTS).rearrange("p (t s) -> p t s", t=TT)
        sel_w = part(TT * SLOTS).rearrange("p (t s) -> p t s", t=TT)
        sel_t = part(TT * SLOTS).rearrange("p (t s) -> p t s", t=TT)
        h2_flat = part(TT * D)
        h2 = h2_flat.rearrange("p (t c n) -> p t c n", t=TT, c=DC)
        wT = part(4 * T).rearrange("p (s t) -> p s t", s=4)
        xblk = part(2 * DC * W).rearrange("p (b c s) -> p b c s", b=2, c=DC)
        th = h2_flat[:, 0:512].rearrange("p (b n) -> p b n", b=2)
        sw = h2_flat[:, 512:1024].rearrange("p (b n) -> p b n", b=2)
        hs = h2_flat[:, 1024:1536].rearrange("p (b n) -> p b n", b=2)
        hx = h2_flat[:, 1536:2048].rearrange("p (b n) -> p b n", b=2)
        yb = sel_s.rearrange("p t s -> p (t s)").rearrange("p (b n) -> p b n", b=2)
        rt = part(24 * TT * NE).rearrange("p (r n) -> p r n", r=24)
        yd = work[:, 0:4 * D].rearrange("p (s d) -> p s d", s=4)
        xin = work[:, 0:TT * D].rearrange("p (t d) -> p t d", t=TT)
        fin = work[:, 4096:4096 + TT * D].rearrange("p (t n c) -> p t n c", t=TT, c=DC)

        ident = con[:, C_ID:C_ID + P]
        ones = con[:, C_ONE:C_ONE + P]
        upper = con[:, C_UP:C_UP + P]
        iota = con[:, C_IOTA:C_IOTA + SLOTS]
        desc = con[:, C_DESC:C_DESC + EG]

        bank = [ctx.enter_context(nc.psum_tensor(f"bank{b}", [P, 512], F32)) for b in range(8)]
        ada_ps = bank[7]

        def ps(g):
            return bank[place[g][0]]

        landed = [sem(f"weights_landed{s}") for s in range(RING)]
        s_third = [sem("third_gate_landed"), sem("third_up_landed")]
        full = [sem(f"bank_full{b}") for b in range(NBANK)]
        s_in = [sem(f"input_landed{n}") for n in range(12)]
        s_xT = sem("xT_chunk_ready")
        s_cexp = sem("cond_tanh")
        s_cond = sem("cond_ready")
        s_ada = sem("ada_item_used")
        s_c32 = sem("cond_copies_ready")
        s_arow = sem("ada_rows_copied")
        s_acol = sem("ada_columns_landed")
        s_kz = sem("key_zeros_ready")
        s_wz = sem("router_zeros_ready")
        s_mod = sem("mod_ready")
        s_sq = sem("squares_ready")
        s_ms = sem("mean_square_taken")
        s_diag = sem("rstd_diag_ready")
        s_hn = sem("h_normed")
        s_h = sem("h_ready")
        s_z = sem("z_copied")
        s_zq = sem("qk_roped")
        s_qT = sem("qkT_ready")
        s_smx = sem("scores_masked")
        s_nm = sem("neg_max_ready")
        s_exp = sem("probs_ready")
        s_pv = sem("values_done")
        s_pT = sem("probsT_ready")
        s_pn = sem("probs_normalised")
        s_yT = sem("branchT_quad_ready")
        s_g = sem("gate_tanh_ready")
        s_ma = sem("branch_a_gated")
        s_mb = sem("branch_b_gated")
        s_m = sem("merged_ready")
        s_out0 = sem("w_out_first_half_used")
        s_x1 = sem("x_after_mixer")
        s_rmax = sem("router_max_ready")
        s_rexp = sem("router_exp_ready")
        s_sel = sem("selection_ready")
        s_cnt = sem("counts_copied")
        s_start = sem("starts_copied")
        s_tab = sem("table_ready")
        s_slot = sem("slots_taken")
        s_S = sem("gather_matrix_ready")
        s_Wm = sem("combine_matrix_ready")
        s_h2 = sem("h_token_major_ready")
        s_pad = sem("xs_pad_cleared")
        s_xsa = sem("xs_even_ready")
        s_xsv = sem("xs_odd_ready")
        s_wT = sem("combineT_ready")
        s_xb = sem("expert_tokens_ready")
        s_gd = sem("expert_gate_done")
        s_ud = sem("expert_up_done")
        s_yd = sem("expert_down_done")
        s_th = sem("expert_tanh_ready")
        s_sw = sem("expert_swish_ready")
        s_hb = sem("expert_hidden_ready")
        s_hd = sem("expert_hidden_transposed")
        s_hx = sem("expert_hiddenT_ready")
        s_yc = sem("expert_result_copied")
        s_yt = sem("expert_result_transposed")
        s_ys = sem("expert_result_stored")
        s_yea = sem("results_even_copied")
        s_yev = sem("results_odd_copied")
        s_x2 = sem("x_after_experts")
        s_fin = sem("output_even_ready")
        s_fin2 = sem("output_odd_ready")
        s_out = sem("output_stored")
        s_link = sem("dve_step")
        fb = [{n: sem(f"over{l}_{n}") for n in ("landed", "x", "up", "tanh", "swish", "h", "hd", "hx", "down", "yc", "yt", "ys")}
              for l in range(DEPTH)]

        XC = [s_xsa, s_xsv]

        def released(g):
            k, r = g[0], g[1:]
            if k == "XT":
                return [(s_xT, r[0] + 1)]
            if k == "FIN":
                return [((s_fin, s_fin2)[r[0] % 2], r[0] // 2 + 1)]
            if k == "AC":
                return [(s_mod, 1)]
            l = r[0]
            if k == "MS":
                return [(s_ms, 2 * l + r[1] + 1)]
            if k == "RB":
                return [(s_hn, DC * (2 * l + r[1] + 1))]
            if k == "Z":
                return [(s_z, 10 * l + ZN.index(r[1:]) + 1)]
            if k == "QT":
                return [(s_qT, 8 * l + QN.index(r[1:]) + 1)]
            if k == "S":
                return [(s_exp, NH * l + r[1] + 1)]
            if k == "PT":
                return [(s_pT, NH * l + r[1] + 1)]
            if k == "G":
                return [(s_g, 8 * l + r[1] + 1)]
            if k == "O":
                return [(s_yT, 4 * l + r[1] + 1)]
            if k == "PA":
                return [(s_ma, 4 * l + r[1] + 1)]
            if k == "PB":
                return [(s_mb, 4 * l + r[1] + 1)]
            if k == "OUT":
                return [(s_x1, 8 * l + 2 * r[1] + 2)]
            if k == "RT":
                return [(s_rexp, l + 1)]
            if k == "H2":
                return [(s_h2, 4 * l + r[1] + 1)]
            if k == "CNT":
                return [(s_cnt, l + 1)]
            if k == "START":
                return [(s_tab, l + 1)]
            if k == "POS":
                return [(s_slot, l + 1)]
            if k == "XS":
                return [(XC[r[1] % 2], 4 * l + r[1] // 2 + 1)]
            if k == "WT":
                return [(s_wT, 2 * l + r[1] + 1)]
            if k == "MOE":
                return [(s_ys, NE * (l + 1))]
            if k == "YS":
                return [((s_yea, s_yev)[r[1] % 2], 4 * l + r[1] // 2 + 1)]
            assert k == "CMB"
            return [(s_x2, 8 * l + 2 * r[1] + 2)]

        def bank_wait(pe, g):
            for o in before[g]:
                for s, v in released(o):
                    pe.wait_ge(s, v)

        def full_wait(eng, g):
            b, v = place[g]
            eng.wait_ge(full[b], v)

        def full_inc(ins, g):
            ins.then_inc(full[place[g][0]], 1)

        def used(it):
            k = it[0]
            if k == "ada":
                return s_ada, it[1] + 1
            l = it[1]
            if k in ("wg", "wu", "wd"):
                return {"wg": s_gd, "wu": s_ud, "wd": s_yd}[k], NE * l + it[2] + 1
            if k == "out" and it[2] == 0:
                return s_out0, l + 1
            g = {"z": lambda: ("Z", l, it[2], TT - 1), "gate": lambda: ("G", l, 2 * it[2] + 1),
                 "pa": lambda: ("PA", l, 3), "pb": lambda: ("PB", l, 3), "out": lambda: ("OUT", l, 3)}[k]()
            b, v = place[g]
            return full[b], v

        def slot_of(it):
            return index[it] % RING

        def weights_wait(eng, it):
            n = index[it]
            eng.wait_ge(landed[n % RING], 16 * (n // RING + 1))

        def rows_8p(w):
            return w.rearrange("(p c) n -> p c n", p=P)

        def rows_128c(w):
            return w.rearrange("(c p) n -> p c n", p=P)

        def expert_src(k, l, e):
            w = {"wg": w_gate, "wu": w_up, "wd": w_down}[k][l]
            w = w[e] if isinstance(e, int) else w[bass.ds(e, 1)].rearrange("a r n -> (a r) n")
            return rows_128c(w) if k == "wd" else rows_8p(w)

        def load(eng, it):
            k = it[0]
            s = slot_of(it)
            buf = ring[:, s, :]
            if k == "ada":
                l, jp, cp = ADA[it[1]]
                src = rows_8p(w_ada[l])[:, 2 * cp:2 * cp + 2, 2 * jp * D:2 * (jp + 1) * D]
                dst = buf.rearrange("p (c n) -> p c n", c=2)
            elif k == "z":
                a, n = Z_COLS[it[2]]
                src = rows_8p(w_in[it[1]])[:, :, a:a + n]
                dst = buf[:, 0:DC * n].rearrange("p (c n) -> p c n", c=DC)
            elif k == "gate":
                a = GATE_COL + it[2] * 512
                src = rows_8p(w_in[it[1]])[:, :, a:a + 512]
                dst = buf.rearrange("p (c n) -> p c n", c=DC)
            elif k in ("pa", "pb"):
                src = rows_128c((w_pa if k == "pa" else w_pb)[it[1]])
                dst = buf.rearrange("p (c n) -> p c n", c=4)
            elif k == "out":
                src = rows_128c(w_out[it[1]])[:, 4 * it[2]:4 * it[2] + 4, :]
                dst = buf.rearrange("p (c n) -> p c n", c=4)
            else:
                src = expert_src(*it)
                dst = buf.rearrange("p (c n) -> p c n", c=4 if k == "wd" else DC)
            eng.dma_start(dst, src).then_inc(landed[s], 16)

        small = [
            (xin[:, :, :], x[0].rearrange("(t p) d -> p t d", p=P)),
            (con[:, 0:C_MASK], const[:, 0:C_MASK]),
            (c_sb[:, :], c[0].rearrange("(p c) -> p c", p=P)),
            (b_sb[:, :, :, :], b_ada.rearrange("l (j p c) -> p l j c", j=6, p=P)),
            (g_sb[:, 0], g_mix.rearrange("l (p c) -> p l c", p=P)),
            (g_sb[:, 1], g_ffn.rearrange("l (p c) -> p l c", p=P)),
            (con[:, C_MASK:NCONST], const[:, C_MASK:NCONST]),
            (qk_gain[:, 0], qn_a.partition_broadcast(P)),
            (qk_gain[:, 1], kn_a.partition_broadcast(P)),
            (qk_gain[:, 2], qn_b.partition_broadcast(P)),
            (qk_gain[:, 3], kn_b.partition_broadcast(P)),
            (wr_sb[:, 0:DC, :], w_router.rearrange("(p c) e -> p c e", p=P)),
        ]
        IN_X, IN_CON, IN_C, IN_B, IN_G, IN_TAB, IN_QK, IN_WR = 0, 1, 2, 3, 4, 6, 7, 11

        block = ctx.enter_context(nc.Block())

        @block.sync
        def _(sp):
            def stream(n):
                if n >= RING:
                    sp.wait_ge(*used(items[n - RING]))
                load(sp, items[n])

            for n in range(IN_TAB):
                sp.dma_start(*small[n]).then_inc(s_in[n], 16)
            n = 0
            for l in range(DEPTH):
                first = index[("wg", l, 0)]
                while n < first + 6:
                    stream(n)
                    n += 1
                full_wait(sp, ("S", l, NH - 1))
                sp.dma_start(third_gate.rearrange("p (c n) -> p c n", c=DC), expert_src("wg", l, 2)).then_inc(s_third[0], 16)
                if l:
                    sp.wait_ge(s_ud, NE * (l - 1) + 3)
                sp.dma_start(third_up.rearrange("p (c n) -> p c n", c=DC), expert_src("wu", l, 2)).then_inc(s_third[1], 16)
                first += 6
                while n < first + 6:
                    stream(n)
                    n += 1
                with sp.Fori(2, NE // 2 - 1) as i:
                    for j in range(6):
                        k, _, e0 = items[first + j]
                        e0 -= 2
                        sp.wait_ge(used((k, l, e0))[0], i * 2 + (NE * l + e0 - 1))
                        s = (first + j) % RING
                        sp.dma_start(ring[:, s, :].rearrange("p (c n) -> p c n", c=4 if k == "wd" else DC),
                                     expert_src(k, l, i * 2 + e0)).then_inc(landed[s], 16)
                n = first + 6 * (NE // 2 - 2)
                while n <= index[("wd", l, NE - 1)]:
                    stream(n)
                    n += 1
                sp.wait_ge(s_tab, l + 1)
                count = sp.value_load(tables[l][0:1, NBLK * NE:NBLK * NE + 1], min_val=0, max_val=T)
                with sp.If(count > overflow_at):
                    f = fb[l]
                    with sp.Fori(0, NE) as e:
                        sp.wait_ge(f["down"], e * NBLK + 1)
                        for j, k in enumerate(("wg", "wu", "wd")):
                            sp.dma_start(ring[:, j, :].rearrange("p (c n) -> p c n", c=4 if k == "wd" else DC),
                                         expert_src(k, l, e)).then_inc(f["landed"], 16)
                    sp.wait_ge(f["down"], NE * NBLK + 1)
            sp.wait_ge(s_out, 16 * TT)

        @block.gpsimd
        def _(pool):
            pool.memset(wr_sb[:, DC:DC + 3, :], 0.0).then_inc(s_wz, 1)

            for l in range(DEPTH):
                if l == 0:
                    pool.wait_ge(s_xT, 4)
                else:
                    pool.wait_ge(s_x2, 8 * l)
                pool.memset(kz[:, :, :, :], 0.0).then_inc(s_kz, 1)
                pool.wait_ge(s_x1, 8 * (l + 1))
                pool.memset(xs[:, :, SLOTS:SPAD], 0.0).then_inc(s_pad, 1)
                pool.wait_ge(s_pad, l + 1)
                for cc in range(DC):
                    pool.wait_ge(XC[cc % 2], 4 * l + cc // 2 + 1)
                    ins = pool.tensor_copy(xblk[:, 0, cc, :], xs[:, cc, 0:W])
                ins.then_inc(s_xb, 1)
                pool.wait_ge(s_tab, l + 1)

                def tokens(e, j, steady):
                    if steady:
                        pool.wait_ge(s_ud, e + (NE * l - 1))
                    first = pool.value_load(tables[l][0:1, bass.ds(e, 1)] if steady else tables[l][0:1, e:e + 1],
                                            min_val=0, max_val=SLOTS)
                    pool.tensor_copy(xblk[:, j], xs[:, :, bass.ds(first, W)]).then_inc(s_xb, 1)

                tokens(1, 1, False)
                with pool.Fori(1, NE // 2) as i:
                    for j in range(2):
                        tokens(i * 2 + j, j, True)
                count = pool.value_load(tables[l][0:1, NBLK * NE:NBLK * NE + 1], min_val=0, max_val=T)
                with pool.If(count > overflow_at):
                    f = fb[l]
                    pool.wait_ge(s_ud, NE * (l + 1))
                    with pool.Fori(0, NE) as e:
                        for b in range(NBLK):
                            pool.wait_ge(f["up"], e * NBLK + (b + 1))
                            first = pool.value_load(tables[l][0:1, bass.ds(e + b * NE, 1)], min_val=0, max_val=SLOTS)
                            pool.tensor_copy(xblk[:, 0], xs[:, :, bass.ds(first, W)]).then_inc(f["x"], 1)

        @block.scalar
        def _(act):
            for n, (dst, src) in enumerate(small):
                if n >= IN_TAB:
                    act.dma_start(dst, src).then_inc(s_in[n], 16)
            act.wait_ge(s_in[IN_C], 16)
            act.activation(cond[:, :], c_sb[:, :], ACT.Tanh, scale=0.5).then_inc(s_cexp, 1)
            for q in range(4):
                full_wait(act, ("XT", q))
                act.activation(xT[:, 2 * q:2 * q + 2, :], ps(("XT", q))[:, :].rearrange("p (c t) -> p c t", c=2),
                               ACT.Copy).then_inc(s_xT, 1)

            def ada_columns(b):
                l, jp = ADA[4 * b][:2]
                act.wait_ge(s_arow, b + 1)
                for q in range(4):
                    act.dma_start(modraw[64 * (q % 2):64 * (q % 2) + 64, l, 2 * jp + q // 2, :],
                                  adarow[32 * q:32 * q + 1, :].rearrange("a (p c) -> a p c", c=DC)).then_inc(s_acol, 16)

            def squares(l, w):
                for cc in range(DC):
                    if w:
                        act.wait_ge(s_x1, 8 * l + cc + 1)
                    elif l:
                        act.wait_ge(s_x2, 8 * (l - 1) + cc + 1)
                    elif cc == 0:
                        act.wait_ge(s_xT, 4)
                    act.activation(hT[:, cc, :], xT[:, cc, :], ACT.Square).then_inc(s_sq, 1)

            def modulate(l, w):
                act.wait_ge(s_mod, 3 * l + 2 * w + 1)
                for cc in range(DC):
                    act.wait_ge(s_hn, DC * (2 * l + w) + cc + 1)
                    act.activation(hT[:, cc, :], hT[:, cc, :], ACT.Identity, bias=mod[:, l, 3 * w, cc:cc + 1],
                                   scale=mscale[:, l, w, cc:cc + 1]).then_inc(s_h, 1)

            def z_out(l, n):
                k, t = ZN[n]
                g = ("Z", l, k, t)
                full_wait(act, g)
                if k == "va":
                    act.activation(va[:, t, :], ps(g)[:, :], ACT.Copy).then_inc(s_z, 1)
                    return
                q = 8 * l + QN.index((k, t))
                if q >= 2:
                    act.wait_ge(s_zq, q - 1)
                m = 128 if k == "kb" else 512
                if k == "kb":
                    act.activation(vb[:, t, :], ps(g)[:, 128:256], ACT.Copy)
                act.activation(zsq[:, q % 2, 0:m], ps(g)[:, 0:m], ACT.Square)
                act.activation(zraw[:, q % 2, 0:m], ps(g)[:, 0:m], ACT.Copy).then_inc(s_z, 1)

            def qT_out(l, k, t):
                g = ("QT", l, k, t)
                n = 2 if k == "kb" else 4
                full_wait(act, g)
                src = ps(g)[:, 0:n * P].rearrange("p (c t) -> p c t", c=n)
                cols = slice(t * P, (t + 1) * P)
                if k in ("qa", "qb"):
                    act.activation(qT[k][:, :, cols], src, ACT.Copy).then_inc(s_qT, 1)
                else:
                    act.wait_ge(s_kz, l + 1)
                    act.activation(kT[k][0:64, :, 0, cols], src[0:64], ACT.Copy)
                    act.activation(kT[k][64:128, :, 1, cols], src[64:128], ACT.Copy).then_inc(s_qT, 1)

            def exps(l, h):
                b = h % 2
                act.wait_ge(s_nm, NH * l + h + 1)
                if h >= 2:
                    full_wait(act, ("PT", l, h - 2))
                for t in range(TT):
                    src = sm[:, b, t, :] if h < HA else ps(("S", l, h))[:, t * T:(t + 1) * T]
                    ins = act.activation(pr[:, b, t, :], src, ACT.Exp, bias=nmax[:, b, t:t + 1], scale=QSCALE,
                                         accum_out=den[:, b, t:t + 1])
                ins.then_inc(s_exp, 1)

            def pT_out(l, h):
                g = ("PT", l, h)
                full_wait(act, g)
                if h >= 2 and (h - 2) % 4 >= 2:
                    full_wait(act, ("O", l, (h - 2) // 4))
                elif h >= 2:
                    act.wait_ge(s_pv, 4 * l + (h - 2) // 4 + 1)
                act.activation(pT[:, h % 2], ps(g)[:, :].rearrange("p (s t) -> p s t", s=TT), ACT.Copy).then_inc(s_pT, 1)

            def gates(l, p):
                g = ("G", l, p)
                full_wait(act, g)
                act.activation(gth[:, p // 4, 2 * (p % 4):2 * (p % 4) + 2, :],
                               ps(g)[:, :].rearrange("p (c t) -> p c t", c=2), ACT.Tanh, scale=0.5).then_inc(s_g, 1)

            def yT_out(l, q):
                g = ("O", l, q)
                full_wait(act, g)
                act.activation(yT[:, q // 2, 2 * (q % 2):2 * (q % 2) + 2, :],
                               ps(g)[:, :].rearrange("p (c t) -> p c t", c=2), ACT.Copy).then_inc(s_yT, 1)

            for l in range(DEPTH):
                squares(l, 0)
                modulate(l, 0)
                for n, k in enumerate(Z_KINDS):
                    for t in range(TT):
                        z_out(l, n * TT + t)
                    if n:
                        for t in range(TT):
                            qT_out(l, Z_KINDS[n - 1], t)
                for h in range(NH + 1):
                    if h < NH:
                        exps(l, h)
                    if h >= 1:
                        pT_out(l, h - 1)
                    if h < NH:
                        for f in filler(l, h):
                            if f[0] == "gate" and f[1] % 2 == 1:
                                gates(l, f[1] // 2)
                    for b in rows_taken(l, h - 1):
                        ada_columns(b)
                    if h >= 4 and h % 4 == 0:
                        yT_out(l, h // 4 - 1)
                squares(l, 1)
                modulate(l, 1)
                act.wait_ge(s_rmax, l + 1)
                for t in range(TT):
                    ins = act.activation(rt[:, 0, t * NE:(t + 1) * NE], ps(("RT", l))[:, t * P:t * P + NE], ACT.Exp,
                                         bias=rt[:, 1, t:t + 1], scale=1.0, accum_out=rt[:, 2, t:t + 1])
                ins.then_inc(s_rexp, 1)
                for q in range(4):
                    g = ("H2", l, q)
                    full_wait(act, g)
                    act.activation(h2[:, q // 2, 4 * (q % 2):4 * (q % 2) + 4, :],
                                   ps(g)[:, :].rearrange("p (c n) -> p c n", c=4), ACT.Copy).then_inc(s_h2, 1)
                for cc in range(0, DC, 2):
                    g = ("XS", l, cc)
                    full_wait(act, g)
                    act.activation(xs[:, cc, 0:SLOTS], ps(g)[:, :], ACT.Copy).then_inc(s_xsa, 1)
                for q in range(2):
                    g = ("WT", l, q)
                    full_wait(act, g)
                    act.activation(wT[:, 2 * q:2 * q + 2, :], ps(g)[:, :].rearrange("p (s t) -> p s t", s=2),
                                   ACT.Copy).then_inc(s_wT, 1)

                act.wait_ge(s_tab, l + 1)

                def tanh_gate(e, j, s_done, s_tanh):
                    act.wait_ge(s_done, e + 1)
                    act.activation(th[:, j], bank[j][:, 0:256], ACT.Tanh, scale=0.5).then_inc(s_tanh, 1)

                def hidden_T(e, j, s_done, s_ready):
                    act.wait_ge(s_done, e + 1)
                    act.activation(hx[:, j], bank[2 + j][:, 0:256], ACT.Copy).then_inc(s_ready, 1)

                def store(row, e, j, s_done, s_stored, bias=0):
                    first = act.value_load(row, min_val=0, max_val=SLOTS)
                    act.wait_ge(s_done, e + 1)
                    act.wait_ge(s_stored, e + bias)
                    act.activation(ys[:, :, bass.ds(first, W)].rearrange("p (j u) s -> p u j s", j=2),
                                   bank[6 + j][:, :].rearrange("p (u j s) -> p u j s", u=4, j=2),
                                   ACT.Copy).then_inc(s_stored, 1)

                def row(e):
                    return tables[l][0:1, e:e + 1] if isinstance(e, int) else tables[l][0:1, bass.ds(e, 1)]

                def step(e, j):
                    n = e + NE * l
                    if not isinstance(e, int) or e < NE:
                        tanh_gate(n, j, s_ud, s_th)
                    if not isinstance(e, int) or e >= 2:
                        store(row(e - 2), n - 2, j, s_yt, s_ys)
                    if not isinstance(e, int) or e < NE:
                        hidden_T(n, j, s_hd, s_hx)

                for e in range(4):
                    step(e, e % 2)
                with act.Fori(2, NE // 2) as i:
                    for j in range(2):
                        step(i * 2 + j, j)
                for e in (NE, NE + 1):
                    step(e, e % 2)
                count = act.value_load(tables[l][0:1, NBLK * NE:NBLK * NE + 1], min_val=0, max_val=T)
                with act.If(count > overflow_at):
                    f = fb[l]
                    act.wait_ge(s_ys, NE * (l + 1))
                    act.sem_inc(f["ys"], 1)
                    with act.Fori(0, NE) as e:
                        for b in range(NBLK):
                            n = e * NBLK + b
                            tanh_gate(n + 1, 0, f["up"], f["tanh"])
                            hidden_T(n, 0, f["hd"], f["hx"])
                            store(row(e + b * NE), n, 0, f["yt"], f["ys"], 1)
                    act.wait_ge(f["ys"], NE * NBLK + 1)
                for q in range(0, 8, 2):
                    g = ("YS", l, q)
                    full_wait(act, g)
                    act.activation(yd[:, q // 2, 0:512], ps(g)[:, :], ACT.Copy).then_inc(s_yea, 1)
            for q in range(0, 4, 2):
                g = ("FIN", q)
                full_wait(act, g)
                act.activation(fin[:, q // 2, :, 4 * (q % 2):4 * (q % 2) + 4].rearrange("p n c -> p c n"),
                               ps(g)[:, :].rearrange("p (c n) -> p c n", c=4), ACT.Copy).then_inc(s_fin, 1)
            for t in range(TT):
                act.wait_ge(s_fin, t + 1)
                act.wait_ge(s_fin2, t + 1)
                act.dma_start(out[0, t * P:(t + 1) * P], work[:, 4096 + t * D:4096 + (t + 1) * D]).then_inc(s_out, 16)
            act.wait_ge(s_out, 16 * TT)

        @block.vector
        def _(dve):
            steps = [0]

            def link(ins):
                steps[0] += 1
                ins.then_inc(s_link, 1)
                dve.wait_ge(s_link, steps[0])

            def inv_sqrt(n):
                v, y, nh, t = nw[:, 0, 0:n], rstd[:, 0:n], nw[:, 1, 0:n], nw[:, 2, 0:n]
                link(dve.tensor_scalar(t.bitcast(I32), v.bitcast(I32), 1, None, ALU.logical_shift_right))
                link(dve.tensor_scalar(y.bitcast(I32), t.bitcast(I32), -1.0, RSQRT_MAGIC, ALU.mult, ALU.add))
                dve.tensor_scalar(nh, v, -0.5, None, ALU.mult)
                for _ in range(3):
                    link(dve.tensor_tensor(t, y, y, ALU.mult))
                    link(dve.tensor_tensor(t, t, nh, ALU.mult))
                    link(dve.scalar_tensor_tensor(y, t, 1.5, y, ALU.add, ALU.mult))

            dve.wait_ge(s_in[IN_C], 16)
            dve.wait_ge(s_cexp, 1)
            link(dve.scalar_tensor_tensor(cond[:, :], cond[:, :], 1.0, c_sb[:, :], ALU.add, ALU.mult))
            dve.tensor_scalar(cond[:, :], cond[:, :], 0.5, None, ALU.mult).then_inc(s_cond, 1)
            dve.wait_ge(s_cond, 1)
            dve.tensor_copy(cond32[:, :, :], cond[:, :].unsqueeze(2).to_broadcast([P, DC, 32])).then_inc(s_c32, 1)

            def take_rows(b):
                dve.wait_ge(s_ada, 4 * (b + 1))
                if b >= 2:
                    dve.wait_ge(s_acol, 64 * (b - 1))
                if b == 1:
                    full_wait(dve, ("AC",))
                dve.tensor_copy(adarow[:, :], ada_ps[:, :]).then_inc(s_arow, 1)

            def take_mod(b):
                l, jp = ADA[4 * b][:2]
                dve.wait_ge(s_in[IN_B], 16)
                if b == 0:
                    full_wait(dve, ("AC",))
                    raw = ps(("AC",))[:, 0:2 * DC].rearrange("p (c j) -> p j c", j=2)
                else:
                    dve.wait_ge(s_acol, 64 * b)
                    raw = modraw[:, l, 2 * jp:2 * jp + 2, :]
                ins = dve.tensor_tensor(mod[:, l, 2 * jp:2 * jp + 2, :], raw, b_sb[:, l, 2 * jp:2 * jp + 2, :], ALU.add)
                link(ins)
                if jp == 1:
                    ins = dve.tensor_scalar(ghalf[:, l], mod[:, l, 2], 0.5, None, ALU.mult)
                else:
                    w = jp // 2
                    dve.wait_ge(s_in[IN_G + w], 16)
                    ins = dve.scalar_tensor_tensor(mscale[:, l, w], mod[:, l, 3 * w + 1], 1.0, g_sb[:, w, l],
                                                   ALU.add, ALU.mult)
                ins.then_inc(s_mod, 1)

            def norm(l, w):
                g = ("MS", l, w)
                full_wait(dve, g)
                dve.tensor_scalar(nw[:, 0, 0:TT], ps(g)[:, 0:TT * P:P], 1.0 / D, EPS, ALU.mult, ALU.add).then_inc(s_ms, 1)
                dve.wait_ge(s_ms, 2 * l + w + 1)
                inv_sqrt(TT)
                dve.wait_ge(s_in[IN_CON], 16)
                for t in range(TT):
                    ins = dve.tensor_scalar(diag[:, t, :], ident, rstd[:, t:t + 1], None, ALU.mult)
                ins.then_inc(s_diag, 1)
                g = ("RB", l, w)
                full_wait(dve, g)
                for cc in range(DC):
                    dve.tensor_tensor(hT[:, cc, :], xT[:, cc, :], ps(g)[:, 0:T], ALU.mult).then_inc(s_hn, 1)
                if w == 0 and l == 0:
                    take_rows(0)
                    take_mod(0)

            def qk(l, k, t):
                q = 8 * l + QN.index((k, t))
                b = q % 2
                heads = 2 if k == "kb" else HA
                m = heads * E
                dve.wait_ge(s_z, 10 * l + ZN.index((k, t)) + 1)
                raw = zraw[:, b, 0:m].rearrange("p (h e) -> p h e", e=E)
                o = zq[:, b, 0:m].rearrange("p (h e) -> p h e", e=E)
                t1 = ztmp[:, 0, 0:m].rearrange("p (h e) -> p h e", e=E)
                t2 = ztmp[:, 1, 0:m].rearrange("p (h e) -> p h e", e=E)
                link(dve.tensor_reduce(nw[:, 3, 0:heads], zsq[:, b, 0:m].rearrange("p (h e) -> p h e", e=E), AX.X, ALU.add))
                link(dve.tensor_scalar(nw[:, 0, 0:heads], nw[:, 3, 0:heads], 1.0 / E, EPS, ALU.mult, ALU.add))
                inv_sqrt(heads)
                if q % 8 >= 2:
                    full_wait(dve, ("QT", l) + QN[q % 8 - 2])
                rope_all = k in ("qb", "kb")
                link(dve.tensor_tensor(raw, raw, rstd[:, 0:heads].unsqueeze(2).to_broadcast([P, heads, E]), ALU.mult))
                dve.wait_ge(s_in[IN_TAB], 16)
                dve.wait_ge(s_in[IN_QK + {"qa": 0, "ka": 1, "qb": 2, "kb": 3}[k]], 16)
                gain = qk_gain[:, {"qa": 0, "ka": 1, "qb": 2, "kb": 3}[k], l, :].unsqueeze(1).to_broadcast([P, heads, E])
                if not rope_all:
                    link(dve.tensor_tensor(o, raw, gain, ALU.mult))
                    cos = con[:, C_COSA + t * 16:C_COSA + (t + 1) * 16].unsqueeze(1).to_broadcast([P, heads, 16])
                    sl = con[:, C_SINA + t * 16:C_SINA + t * 16 + 8].unsqueeze(1).to_broadcast([P, heads, 8])
                    sh = con[:, C_SINA + t * 16 + 8:C_SINA + t * 16 + 16].unsqueeze(1).to_broadcast([P, heads, 8])
                    dve.tensor_tensor(t1[:, :, 0:16], o[:, :, 0:16], cos, ALU.mult)
                    dve.tensor_tensor(t2[:, :, 0:8], o[:, :, 8:16], sl, ALU.mult)
                    link(dve.tensor_tensor(t2[:, :, 8:16], o[:, :, 0:8], sh, ALU.mult))
                    dve.tensor_tensor(o[:, :, 0:16], t1[:, :, 0:16], t2[:, :, 0:16], ALU.add).then_inc(s_zq, 1)
                else:
                    link(dve.tensor_tensor(raw, raw, gain, ALU.mult))
                    cos = con[:, C_COSB + t * E:C_COSB + (t + 1) * E].unsqueeze(1).to_broadcast([P, heads, E])
                    dve.tensor_tensor(t1, raw, cos, ALU.mult)
                    for a in range(2):
                        c0 = C_SINB + t * E + a * 32
                        for half in range(2):
                            s = con[:, c0 + half * 16:c0 + half * 16 + 16].unsqueeze(1).to_broadcast([P, heads, 16])
                            lo, hi = a * 32 + half * 16, a * 32 + (1 - half) * 16
                            ins = dve.tensor_tensor(t2[:, :, lo:lo + 16], raw[:, :, hi:hi + 16], s, ALU.mult)
                    link(ins)
                    if k == "qb":
                        dve.tensor_tensor(o, t1, t2, ALU.add).then_inc(s_zq, 1)
                    else:
                        o2 = zq[:, b, 0:2 * m].rearrange("p (h d e) -> p h d e", d=2, e=E)
                        dve.tensor_tensor(o2[:, :, 0, :], t1, t2, ALU.add)
                        dve.tensor_tensor(o2[:, :, 1, :], t1, t2, ALU.add).then_inc(s_zq, 1)

            def head_max(l, h):
                n = NH * l + h
                b = h % 2
                g = ("S", l, h)
                full_wait(dve, g)
                if h >= 2:
                    dve.wait_ge(s_exp, n - 1)
                if h < HA:
                    for t in range(TT):
                        ins = dve.tensor_tensor_reduce(
                            out=sm[:, b, t, :], in0=ps(g)[:, t * T:(t + 1) * T],
                            in1=con[:, C_MASK + t * T:C_MASK + (t + 1) * T], scale=1.0, scalar=-3e38,
                            op0=ALU.add, op1=ALU.max, accum_out=mx[:, b, t:t + 1])
                    link(ins)
                else:
                    link(dve.tensor_reduce(mx[:, b, :], ps(g)[:, :].rearrange("p (t s) -> p t s", t=TT), AX.X, ALU.max))
                dve.tensor_scalar(nmax[:, b, :], mx[:, b, :], -QSCALE, None, ALU.mult).then_inc(s_nm, 1)

            def normalise(l, h):
                b = h % 2
                dve.wait_ge(s_exp, NH * l + h + 1)
                link(dve.reciprocal(rden[:, b, :], den[:, b, :]))
                for t in range(TT):
                    ins = dve.tensor_scalar(pr[:, b, t, :], pr[:, b, t, :], rden[:, b, t:t + 1], None, ALU.mult)
                ins.then_inc(s_pn, 1)

            def merge(l):
                for q in range(4):
                    g = ("PA", l, q)
                    full_wait(dve, g)
                    if q == 0:
                        dve.wait_ge(s_g, 8 * (l + 1))
                    a = gth[:, 0, 2 * q:2 * q + 2, :]
                    dve.scalar_tensor_tensor(a, a, 1.0, ps(g)[:, :].rearrange("p (c t) -> p c t", c=2),
                                             ALU.add, ALU.mult).then_inc(s_ma, 1)
                for q in range(4):
                    g = ("PB", l, q)
                    full_wait(dve, g)
                    a, b = gth[:, 0, 2 * q:2 * q + 2, :], gth[:, 1, 2 * q:2 * q + 2, :]
                    dve.scalar_tensor_tensor(b, b, 1.0, ps(g)[:, :].rearrange("p (c t) -> p c t", c=2),
                                             ALU.add, ALU.mult).then_inc(s_mb, 1)
                    dve.wait_ge(s_mb, 4 * l + q + 1)
                    dve.wait_ge(s_ma, 4 * l + q + 1)
                    dve.tensor_tensor(a, a, b, ALU.add).then_inc(s_m, 1)

            def residual(l, name, gate, s):
                for cc in range(DC):
                    g = (name, l, cc // 2)
                    full_wait(dve, g)
                    dve.scalar_tensor_tensor(xT[:, cc, :], ps(g)[:, (cc % 2) * T:(cc % 2 + 1) * T], gate[:, cc:cc + 1],
                                             xT[:, cc, :], ALU.mult, ALU.add).then_inc(s, 1)

            def route(l):
                g = ("RT", l)
                prob = rt[:, 0, :]
                tg = lambda r: rt[:, r, :].rearrange("p (g j) -> p g j", j=EG)
                col = lambda r: rt[:, r, 0:TT * NG]
                bc = lambda r: col(r).unsqueeze(2).to_broadcast([P, TT * NG, EG])
                grp = lambda r: col(r).rearrange("p (t g) -> p t g", t=TT)
                full_wait(dve, g)
                link(dve.tensor_reduce(rt[:, 3, 0:TT], ps(g)[:, 0:TT * P].rearrange("p (t n) -> p t n", t=TT)[:, :, 0:NE],
                                       AX.X, ALU.max))
                dve.tensor_scalar(rt[:, 1, 0:TT], rt[:, 3, 0:TT], -1.0, None, ALU.mult).then_inc(s_rmax, 1)
                dve.wait_ge(s_rexp, l + 1)
                link(dve.reciprocal(rt[:, 3, 0:TT], rt[:, 2, 0:TT]))
                link(dve.tensor_tensor(prob.rearrange("p (t e) -> p t e", t=TT), prob.rearrange("p (t e) -> p t e", t=TT),
                                       rt[:, 3, 0:TT].unsqueeze(2).to_broadcast([P, TT, NE]), ALU.mult))
                d = desc.unsqueeze(1).to_broadcast([P, TT * NG, EG])

                def first_max(src, best, onehot):
                    link(dve.tensor_reduce(col(best), tg(src), AX.X, ALU.max))
                    link(dve.tensor_tensor(tg(4), tg(src), bc(best), ALU.is_equal))
                    link(dve.tensor_tensor(tg(4), tg(4), d, ALU.mult))
                    link(dve.tensor_reduce(col(5), tg(4), AX.X, ALU.max))
                    link(dve.tensor_tensor(tg(onehot), tg(4), bc(5), ALU.is_equal))

                first_max(0, 6, 8)
                link(dve.scalar_tensor_tensor(rt[:, 7, :], rt[:, 8, :], -4.0, rt[:, 0, :], ALU.mult, ALU.add))
                first_max(7, 9, 10)
                link(dve.tensor_tensor(col(11), col(6), col(9), ALU.add))
                link(dve.tensor_reduce(rt[:, 12, 0:TT], grp(11), AX.X, ALU.max))
                link(dve.tensor_tensor(grp(13), grp(11), rt[:, 12, 0:TT].unsqueeze(2).to_broadcast([P, TT, NG]), ALU.is_equal))
                link(dve.tensor_tensor(grp(13), grp(13), desc[:, 0:NG].unsqueeze(1).to_broadcast([P, TT, NG]), ALU.mult))
                link(dve.tensor_reduce(rt[:, 12, 0:TT], grp(13), AX.X, ALU.max))
                link(dve.tensor_tensor(grp(14), grp(13), rt[:, 12, 0:TT].unsqueeze(2).to_broadcast([P, TT, NG]), ALU.is_equal))
                link(dve.tensor_tensor(tg(8), tg(8), bc(14), ALU.mult))
                link(dve.tensor_tensor(tg(10), tg(10), bc(14), ALU.mult))
                dve.tensor_tensor(rt[:, 15, :], rt[:, 8, :], rt[:, 10, :], ALU.add).then_inc(s_sel, 1)
                link(dve.reciprocal(col(16), col(11)))
                link(dve.tensor_tensor(col(16), col(16), col(14), ALU.mult))
                dve.tensor_tensor(col(17), col(16), col(6), ALU.mult)
                link(dve.tensor_tensor(col(18), col(16), col(9), ALU.mult))
                dve.tensor_reduce(rt[:, 19, 0:TT], grp(17), AX.X, ALU.add)
                link(dve.tensor_reduce(rt[:, 20, 0:TT], grp(18), AX.X, ALU.add))
                full_wait(dve, ("CNT", l))
                dve.tensor_copy(ccol[:, :], ps(("CNT", l))[0:NE, 0:P]).then_inc(s_cnt, 1)
                full_wait(dve, ("POS", l))
                pos = ps(("POS", l))[:, 0:TT * NE]
                dve.tensor_tensor(rt[:, 4, :], rt[:, 8, :], pos, ALU.mult)
                dve.tensor_tensor(rt[:, 7, :], rt[:, 10, :], pos, ALU.mult).then_inc(s_slot, 1)
                dve.wait_ge(s_slot, l + 1)
                p2 = lambda r: rt[:, r, :].rearrange("p (t e) -> p t e", t=TT)
                dve.tensor_reduce(rt[:, 5, 0:TT], p2(4), AX.X, ALU.add)
                link(dve.tensor_reduce(rt[:, 6, 0:TT], p2(7), AX.X, ALU.add))
                for t in range(TT):
                    link(dve.tensor_scalar(sel_t[:, t], iota, rt[:, 5, t:t + 1], None, ALU.is_equal))
                    dve.scalar_tensor_tensor(sel_s[:, t], iota, rt[:, 6, t:t + 1], sel_t[:, t],
                                             ALU.is_equal, ALU.add).then_inc(s_S, 1)
                full_wait(dve, ("START", l))
                st = ps(("START", l))
                link(dve.tensor_reduce(rt[0:1, 21, 0:1], st[0:1, NE:2 * NE], AX.X, ALU.max))
                link(dve.tensor_copy(tables[l][0:1, NBLK * NE:NBLK * NE + 1], rt[0:1, 21, 0:1]))
                link(dve.tensor_copy(rt[0:1, 22, 0:NE], st[0:1, 0:NE]))
                for b in range(NBLK):
                    ins = dve.tensor_scalar(tables[l][0:1, b * NE:(b + 1) * NE], rt[0:1, 22, 0:NE], float(b * W), float(SLOTS),
                                            ALU.add, ALU.min)
                ins.then_inc(s_tab, 1)
                for t in range(TT):
                    link(dve.tensor_scalar(sel_w[:, t], iota, rt[:, 6, t:t + 1], rt[:, 20, t:t + 1], ALU.is_equal, ALU.mult))
                    dve.scalar_tensor_tensor(sel_w[:, t], sel_t[:, t], rt[:, 19, t:t + 1], sel_w[:, t],
                                             ALU.mult, ALU.add).then_inc(s_Wm, 1)

            def swish(e, j, s_tanh, s_swish, s_hid):
                dve.wait_ge(s_tanh, e + 1)
                dve.scalar_tensor_tensor(sw[:, j], th[:, j], 1.0, bank[j][:, 0:256], ALU.add, ALU.mult).then_inc(s_swish, 1)
                dve.wait_ge(s_swish, e + 1)
                dve.scalar_tensor_tensor(hs[:, j], sw[:, j], 0.5, bank[j][:, 256:512], ALU.mult, ALU.mult).then_inc(s_hid, 1)

            def result(e, j, s_done, s_copied):
                dve.wait_ge(s_done, e + 1)
                dve.tensor_copy(yb[:, j], bank[4 + j][:, :]).then_inc(s_copied, 1)

            for l in range(DEPTH):
                norm(l, 0)
                for k, t in QN:
                    qk(l, k, t)
                for h in range(-1, NH):
                    if h >= 0:
                        head_max(l, h)
                        normalise(l, h)
                    for b in rows_taken(l, h):
                        take_rows(b)
                merge(l)
                for b in BATCHES[l][:2]:
                    take_mod(b)
                dve.wait_ge(s_mod, 3 * l + 2)
                residual(l, "OUT", ghalf[:, l], s_x1)
                norm(l, 1)
                route(l)
                for b in BATCHES[l][2:]:
                    take_mod(b)
                for cc in range(1, DC, 2):
                    g = ("XS", l, cc)
                    full_wait(dve, g)
                    dve.tensor_copy(xs[:, cc, 0:SLOTS], ps(g)[:, :]).then_inc(s_xsv, 1)
                n = NE * l
                swish(n, 0, s_th, s_sw, s_hb)
                for e in range(1, 4):
                    swish(n + e, e % 2, s_th, s_sw, s_hb)
                    result(n + e - 1, (e - 1) % 2, s_yd, s_yc)
                with dve.Fori(2, NE // 2) as i:
                    for j in range(2):
                        swish(i * 2 + (n + j), j, s_th, s_sw, s_hb)
                        result(i * 2 + (n + j - 1), 1 - j, s_yd, s_yc)
                result(n + NE - 1, 1, s_yd, s_yc)
                count = dve.value_load(tables[l][0:1, NBLK * NE:NBLK * NE + 1], min_val=0, max_val=T)
                with dve.If(count > overflow_at):
                    f = fb[l]
                    with dve.Fori(0, NE) as e:
                        for b in range(NBLK):
                            swish(e * NBLK + b, 0, f["tanh"], f["swish"], f["h"])
                            result(e * NBLK + (b + 1), 0, f["down"], f["yc"])
                for q in range(1, 8, 2):
                    g = ("YS", l, q)
                    full_wait(dve, g)
                    dve.tensor_copy(yd[:, q // 2, 512:1024], ps(g)[:, :]).then_inc(s_yev, 1)
                residual(l, "CMB", mod[:, l, 5], s_x2)
            for q in range(1, 4, 2):
                g = ("FIN", q)
                full_wait(dve, g)
                dve.tensor_copy(fin[:, q // 2, :, 4:8].rearrange("p n c -> p c n"),
                                ps(g)[:, :].rearrange("p (c n) -> p c n", c=4)).then_inc(s_fin2, 1)

        @block.tensor
        def _(pe):
            order = iter(psum_groups())

            def begin(g):
                assert next(order) == g, g
                bank_wait(pe, g)

            pe.wait_ge(s_in[IN_X], 16)
            pe.wait_ge(s_in[IN_CON], 16)
            for q in range(4):
                g = ("XT", q)
                begin(g)
                for n in range(4):
                    cc, t = 2 * q + n // 2, n % 2
                    ins = pe.transpose(ps(g)[:, n * P:(n + 1) * P], xin[:, t, cc:D:DC], ident)
                full_inc(ins, g)

            def norm(l, w):
                g = ("MS", l, w)
                begin(g)
                for cc in range(DC):
                    pe.wait_ge(s_sq, 8 * (2 * l + w) + cc + 1)
                    for t in range(TT):
                        ins = pe.matmul(ps(g)[:, t * P:(t + 1) * P], hT[:, cc, t * P:(t + 1) * P], ones,
                                        start=(cc == 0 and t == 0), stop=(cc == DC - 1), skip_group_check=True)
                full_inc(ins, g)
                g = ("RB", l, w)
                begin(g)
                pe.wait_ge(s_diag, 2 * l + w + 1)
                for t in range(TT):
                    ins = pe.matmul(ps(g)[:, t * P:(t + 1) * P], ones, diag[:, t, :], start=True, stop=True)
                full_inc(ins, g)

            def ada(n):
                l, jp, cp = ADA[n]
                if n % 4 == 0 and n:
                    pe.wait_ge(s_arow, n // 4)
                if n == 0:
                    pe.wait_ge(s_c32, 1)
                weights_wait(pe, ("ada", n))
                wt = ring[:, slot_of(("ada", n)), :].rearrange("p (c n) -> p c n", c=2)
                for k in range(2):
                    for q in range(4):
                        ins = pe.matmul(ada_ps[32 * q:32 * q + 32, :], cond32[:, 2 * cp + k, :],
                                        wt[:, k, q * 512:(q + 1) * 512], start=(cp == 0 and k == 0),
                                        stop=(cp == 3 and k == 1), skip_group_check=True)
                ins.then_inc(s_ada, 1)

            def z(l, k):
                it = ("z", l, k)
                n = Z_COLS[k][1]
                wt = ring[:, slot_of(it), 0:DC * n].rearrange("p (c n) -> p c n", c=DC)
                for t in range(TT):
                    g = ("Z", l, k, t)
                    begin(g)
                    if t == 0:
                        weights_wait(pe, it)
                    for cc in range(DC):
                        if t == 0 and k == Z_KINDS[0]:
                            pe.wait_ge(s_h, 16 * l + cc + 1)
                        ins = pe.matmul(ps(g)[:, 0:n], hT[:, cc, t * P:(t + 1) * P], wt[:, cc, :],
                                        start=(cc == 0), stop=(cc == DC - 1))
                    full_inc(ins, g)

            def qk_T(l, k, t):
                q = 8 * l + QN.index((k, t))
                g = ("QT", l, k, t)
                begin(g)
                pe.wait_ge(s_zq, q + 1)
                for n in range(2 if k == "kb" else 4):
                    ins = pe.transpose(ps(g)[:, n * P:(n + 1) * P], zq[:, q % 2, n * P:(n + 1) * P], ident)
                full_inc(ins, g)

            def scores(l, h):
                g = ("S", l, h)
                begin(g)
                if h < HA:
                    pe.wait_ge(s_qT, 8 * l + 4)
                    q, k = qT["qa"][:, h // 2], kT["ka"][:, h // 2, h % 2]
                else:
                    pe.wait_ge(s_qT, 8 * l + 8)
                    q, k = qT["qb"][:, (h - HA) // 2], kT["kb"][:, (h - HA) // 4, h % 2]
                for t in range(TT):
                    ins = pe.matmul(ps(g)[:, t * T:(t + 1) * T], q[:, t * P:(t + 1) * P], k, start=True, stop=True)
                full_inc(ins, g)

            def probs_T(l, h):
                g = ("PT", l, h)
                begin(g)
                pe.wait_ge(s_pn, NH * l + h + 1)
                for s in range(TT):
                    for t in range(TT):
                        ins = pe.transpose(ps(g)[:, (s * TT + t) * P:(s * TT + t + 1) * P],
                                           pr[:, h % 2, t, s * P:(s + 1) * P], ident)
                full_inc(ins, g)

            def values(l, pair):
                g = ("O", l, pair // 2)
                if pair % 2 == 0:
                    begin(g)
                if pair == 0:
                    pe.wait_ge(s_z, 10 * l + ZN.index(("va", TT - 1)) + 1)
                if pair == HA // 2:
                    pe.wait_ge(s_z, 10 * l + ZN.index(("kb", TT - 1)) + 1)
                pe.wait_ge(s_pT, NH * l + 2 * pair + 2)
                for s in range(TT):
                    for u in range(2):
                        h = 2 * pair + u
                        v = va[:, s, h * E:(h + 1) * E] if h < HA else vb[:, s, (h - HA) // 4 * E:((h - HA) // 4 + 1) * E]
                        ins = pe.matmul(ps(g)[64 * u:64 * u + 64, (pair % 2) * T:(pair % 2 + 1) * T], v, pT[:, u, s, :],
                                        start=(pair % 2 == 0 and s == 0), stop=(s == TT - 1), skip_group_check=True)
                if pair % 2:
                    full_inc(ins, g)
                else:
                    ins.then_inc(s_pv, 1)

            def gate(l, m):
                it = ("gate", l, m // 4)
                wt = ring[:, slot_of(it), :].rearrange("p (c n) -> p c n", c=DC)
                g = ("G", l, m // 2)
                if m % 2 == 0:
                    begin(g)
                if m % 4 == 0:
                    weights_wait(pe, it)
                for cc in range(DC):
                    ins = pe.matmul(ps(g)[:, (m % 2) * T:(m % 2 + 1) * T], wt[:, cc, (m % 4) * P:(m % 4 + 1) * P],
                                    hT[:, cc, :], start=(cc == 0), stop=(cc == DC - 1))
                if m % 2:
                    full_inc(ins, g)

            def project(l, name, it, br):
                wt = ring[:, slot_of(it), :].rearrange("p (c n) -> p c n", c=4)
                for q in range(4):
                    g = (name, l, q)
                    begin(g)
                    if q == 0:
                        weights_wait(pe, it)
                        pe.wait_ge(s_yT, 4 * l + 2 * br + 2)
                    for u in range(2):
                        m = 2 * q + u
                        for k in range(4):
                            ins = pe.matmul(ps(g)[:, u * T:(u + 1) * T], wt[:, k, m * P:(m + 1) * P], yT[:, br, k, :],
                                            start=(k == 0), stop=(k == 3))
                    full_inc(ins, g)

            def project_out(l):
                for half in range(2):
                    it = ("out", l, half)
                    weights_wait(pe, it)
                    wt = ring[:, slot_of(it), :].rearrange("p (c n) -> p c n", c=4)
                    for q in range(4):
                        g = ("OUT", l, q)
                        if half == 0:
                            begin(g)
                        for u in range(2):
                            cc = 2 * q + u
                            for k in range(4):
                                if q == 0 and u == 0 and k % 2 == 0:
                                    pe.wait_ge(s_m, 4 * l + (4 * half + k) // 2 + 1)
                                ins = pe.matmul(ps(g)[:, u * T:(u + 1) * T], wt[:, k, cc:D:DC], gth[:, 0, 4 * half + k, :],
                                                start=(half == 0 and u == 0 and k == 0), stop=(half == 1 and k == 3),
                                                skip_group_check=True)
                        if half == 1:
                            full_inc(ins, g)
                    if half == 0:
                        ins.then_inc(s_out0, 1)

            def route(l):
                g = ("RT", l)
                begin(g)
                pe.wait_ge(s_in[IN_WR], 16)
                pe.wait_ge(s_wz, 1)
                for t in range(TT):
                    for cc in range(DC):
                        if t == 0:
                            pe.wait_ge(s_h, 16 * l + DC + cc + 1)
                        ins = pe.matmul(ps(g)[:, t * P:(t + 1) * P], hT[:, cc, t * P:(t + 1) * P], wr_sb[:, cc:cc + 4, :],
                                        start=(cc == 0), stop=(cc == DC - 1))
                full_inc(ins, g)
                for q in range(4):
                    g = ("H2", l, q)
                    begin(g)
                    for n in range(4):
                        t, cc = q // 2, 4 * (q % 2) + n
                        ins = pe.transpose(ps(g)[:, n * P:(n + 1) * P], hT[:, cc, t * P:(t + 1) * P], ident)
                    full_inc(ins, g)
                sel = rt[:, 15, :]
                g = ("CNT", l)
                begin(g)
                pe.wait_ge(s_sel, l + 1)
                for t in range(TT):
                    ins = pe.matmul(ps(g)[0:NE, 0:P], sel[:, t * NE:(t + 1) * NE], ones, start=(t == 0), stop=(t == TT - 1))
                full_inc(ins, g)
                g = ("START", l)
                begin(g)
                for t in range(TT):
                    pe.matmul(ps(g)[:, NE:2 * NE], ones, sel[:, t * NE:(t + 1) * NE], start=(t == 0), stop=(t == TT - 1))
                pe.wait_ge(s_cnt, l + 1)
                ins = pe.matmul(ps(g)[:, 0:NE], ccol[:, :], upper[0:NE, 0:NE], start=True, stop=True)
                full_inc(ins, g)
                g = ("POS", l)
                begin(g)
                pe.matmul(ps(g)[:, 0:NE], upper, sel[:, 0:NE], start=True, stop=False)
                pe.matmul(ps(g)[:, 0:NE], ccol[:, :], upper[0:NE, 0:NE], start=False, stop=True)
                pe.matmul(ps(g)[:, NE:2 * NE], ones, sel[:, 0:NE], start=True, stop=False)
                pe.matmul(ps(g)[:, NE:2 * NE], ccol[:, :], upper[0:NE, 0:NE], start=False, stop=False)
                ins = pe.matmul(ps(g)[:, NE:2 * NE], upper, sel[:, NE:2 * NE], start=False, stop=True)
                full_inc(ins, g)
                for cc in range(DC):
                    g = ("XS", l, cc)
                    begin(g)
                    if cc == 0:
                        pe.wait_ge(s_h2, 4 * l + 4)
                    for t in range(TT):
                        if cc == 0:
                            pe.wait_ge(s_S, TT * l + t + 1)
                        ins = pe.matmul(ps(g)[:, :], h2[:, t, cc, :], sel_s[:, t], start=(t == 0), stop=(t == TT - 1))
                    full_inc(ins, g)
                for q in range(2):
                    g = ("WT", l, q)
                    begin(g)
                    if q == 0:
                        pe.wait_ge(s_Wm, TT * (l + 1))
                    for n in range(4):
                        s, t = 2 * q + n // TT, n % TT
                        ins = pe.transpose(ps(g)[:, n * P:(n + 1) * P], sel_w[:, t, s * P:(s + 1) * P], ident)
                    full_inc(ins, g)

            def gate_up(g, wt, dst, xb, s):
                wv = wt.rearrange("p (c n) -> p c n", c=DC)
                for cc in range(DC):
                    for half in range(2):
                        ins = pe.matmul(dst[64 * half:64 * half + 64, g * 256:g * 256 + 256], xb[:, cc, :],
                                        wv[:, cc, half * 256:half * 256 + 256],
                                        start=(cc == 0 and g == 0), stop=(cc == DC - 1), skip_group_check=True)
                if s is not None:
                    ins.then_inc(s, 1)

            def hidden_T(j, s):
                for v in range(2):
                    ins = pe.transpose(bank[2 + j][:, v * P:(v + 1) * P], hs[:, j, v * P:(v + 1) * P], ident)
                ins.then_inc(s, 1)

            def down(wt, j, s):
                wv = wt.rearrange("p (c n) -> p c n", c=FC)
                for half in range(2):
                    for v in range(2):
                        for out_half in range(2):
                            m = 2 * half + v
                            ins = pe.matmul(bank[4 + j][64 * out_half:64 * out_half + 64, :],
                                            hx[:, j, v * P + 64 * half:v * P + 64 * half + 64],
                                            wv[:, m, out_half * 512:out_half * 512 + 512],
                                            start=(m == 0), stop=(m == FC - 1), skip_group_check=True)
                ins.then_inc(s, 1)

            def result_T(j, s):
                for u in range(4):
                    ins = pe.transpose(bank[6 + j][:, u * P:(u + 1) * P], yb[:, j, u * P:(u + 1) * P], ident)
                ins.then_inc(s, 1)

            def expert(l, i, j):
                e = i * 2 + j
                n = e + NE * l
                known = isinstance(i, int)

                def weights(k, e, i, j):
                    if known and e == 2 and k != "wd":
                        pe.wait_ge(s_third[k == "wu"], 16 * (l + 1))
                        return third_up[:, :] if k == "wu" else third_gate
                    it = index[(k, l, e if known else 4 + j - (k == "wd"))]
                    pe.wait_ge(landed[it % RING], (0 if known else (i - 2) * 16) + 16 * (it // RING + 1))
                    return ring[:, it % RING, :]

                if not known or e < NE:
                    pe.wait_ge(s_xb, n + 1)
                    for g in range(2):
                        gate_up(g, weights(("wg", "wu")[g], e, i, j), bank[j], xblk[:, j], (s_gd, s_ud)[g])
                if not known or e >= 2:
                    pe.wait_ge(s_yc, n - 1)
                    if not known or e >= 4:
                        pe.wait_ge(s_ys, n - 3)
                    result_T(j, s_yt)
                if not known or 1 <= e <= NE:
                    pe.wait_ge(s_hx, n)
                    down(weights("wd", e - 1, i, j), 1 - j, s_yd)
                if not known or e < NE:
                    pe.wait_ge(s_hb, n + 1)
                    hidden_T(j, s_hd)

            def experts(l):
                begin(("MOE", l))
                pe.wait_ge(s_arow, (4, ADA_BATCHES)[l])
                for e in range(4):
                    expert(l, e // 2, e % 2)
                with pe.Fori(2, NE // 2) as i:
                    for j in range(2):
                        expert(l, i, j)
                for e in (NE, NE + 1):
                    expert(l, e // 2, e % 2)
                count = pe.value_load(tables[l][0:1, NBLK * NE:NBLK * NE + 1], min_val=0, max_val=T)
                with pe.If(count > overflow_at):
                    f = fb[l]
                    pe.wait_ge(s_ys, NE * (l + 1))
                    pe.wait_ge(s_ud, NE * (l + 1))
                    pe.sem_inc(f["down"], 1)
                    pe.sem_inc(f["up"], 1)
                    with pe.Fori(0, NE) as e:
                        pe.wait_ge(f["landed"], e * 48 + 48)
                        for b in range(NBLK):
                            n = e * NBLK + (b + 1)
                            pe.wait_ge(f["x"], n)
                            gate_up(0, ring[:, 0, :], bank[0], xblk[:, 0], None)
                            gate_up(1, ring[:, 1, :], bank[0], xblk[:, 0], f["up"])
                            pe.wait_ge(f["h"], n)
                            hidden_T(0, f["hd"])
                            pe.wait_ge(f["hx"], n)
                            down(ring[:, 2, :], 0, f["down"])
                            pe.wait_ge(f["yc"], n)
                            pe.wait_ge(f["ys"], n)
                            result_T(0, f["yt"])
                    pe.wait_ge(f["ys"], NE * NBLK + 1)

            def combine(l):
                for q in range(8):
                    g = ("YS", l, q)
                    begin(g)
                    if q == 0:
                        pe.wait_ge(s_ys, NE * (l + 1))
                    for n in range(4):
                        s, cc = q // 2, 4 * (q % 2) + n
                        ins = pe.transpose(ps(g)[:, n * P:(n + 1) * P], ys[:, cc, s * P:(s + 1) * P], ident)
                    full_inc(ins, g)
                for q in range(4):
                    g = ("CMB", l, q)
                    begin(g)
                    if q == 0:
                        pe.wait_ge(s_yea, 4 * (l + 1))
                        pe.wait_ge(s_yev, 4 * (l + 1))
                        pe.wait_ge(s_wT, 2 * (l + 1))
                    for u in range(2):
                        for s in range(4):
                            ins = pe.matmul(ps(g)[:, u * T:(u + 1) * T], yd[:, s, 2 * q + u:D:DC], wT[:, s, :],
                                            start=(s == 0), stop=(s == 3))
                    full_inc(ins, g)

            norm(0, 0)
            for n in range(4):
                ada(n)
            g = ("AC",)
            begin(g)
            pe.wait_ge(s_arow, 1)
            for cc in range(DC):
                for half in range(2):
                    ins = pe.matmul(ps(g)[64 * half:64 * half + 64, 2 * cc:2 * cc + 2], adarow[:, cc:512:DC],
                                    ident[:, 32 * half:P:64], start=True, stop=True, skip_group_check=True)
            full_inc(ins, g)
            for l in range(DEPTH):
                if l:
                    norm(l, 0)
                for n, k in enumerate(Z_KINDS):
                    z(l, k)
                    if n:
                        for t in range(TT):
                            qk_T(l, Z_KINDS[n - 1], t)
                    for a in z_filler(l, n):
                        ada(a)
                for h in range(NH + 1):
                    if h < NH:
                        scores(l, h)
                    if h >= 1:
                        probs_T(l, h - 1)
                    if h < NH:
                        for f in filler(l, h):
                            if f[0] == "gate":
                                gate(l, f[1])
                            else:
                                ada(f[1])
                    if h >= 2 and h % 2 == 0:
                        values(l, h // 2 - 1)
                project(l, "PA", ("pa", l), 0)
                project(l, "PB", ("pb", l), 1)
                project_out(l)
                norm(l, 1)
                route(l)
                experts(l)
                combine(l)
            for q in range(4):
                g = ("FIN", q)
                begin(g)
                if q == 0:
                    pe.wait_ge(s_x2, 8 * DEPTH)
                for n in range(4):
                    ins = pe.transpose(ps(g)[:, n * P:(n + 1) * P],
                                       xT[:, 4 * (q % 2) + n, (q // 2) * P:(q // 2 + 1) * P], ident)
                full_inc(ins, g)


_INS = ["x", "c", "w_ada", "b_ada", "g_mix", "w_in", "qn_a", "kn_a", "qn_b", "kn_b", "w_pa", "w_pb", "w_out",
        "g_ffn", "w_router", "w_gate", "w_up", "w_down"]


def kernel(**inputs):
    import concourse.bacc as _bacc
    from concourse.bass_utils import run_bass_kernel_spmd as _run

    nc = _bacc.Bacc("TRN2", target_bir_lowering=False, num_devices=1,
                    dynamic_dma_scratch_size=SCRATCH)
    arrays, args = {}, []
    given = [(name, np.ascontiguousarray(inputs[name])) for name in _INS] + [("const", constants())]
    for name, a in given:
        arrays[f"in_{name}_dram"] = a
        args.append(nc.dram_tensor(f"in_{name}_dram", a.shape, mybir.dt.from_np(a.dtype), kind="ExternalInput").ap())
    args.append(nc.dram_tensor("out_0_dram", (1, T, D), F32, kind="ExternalOutput").ap())
    build(nc, *args)
    r = _run(nc, [arrays], core_ids=[0])
    return r.results[0]["out_0_dram"]
```
